# Optimizing a Trainium2 kernel written in Bass

```python
import math
import jax, jax.numpy as jnp
from jax import lax
import numpy as np

D_MODEL = 2048
BATCH = 1
SEQ = 512
DEPTH = 1

A_HEADS = 8
A_HEAD_DIM = 64
A_WIDTH = A_HEADS * 2 * A_HEAD_DIM
B_HEADS = 8
B_HEAD_DIM = 128
B_WIDTH = B_HEADS * B_HEAD_DIM
B_GROUPS = ((128, 1), (512, 4), (2048, 16))
C_WIDTH = 1024
C_CONV = 3
N_BRANCH = 3
Q_BLOCK = 128
N_ALIBI = A_HEADS + len(B_GROUPS) * B_HEADS
RMS_EPS = 1e-6

SPLIT_SIZES = ([A_WIDTH] * 4
               + [B_WIDTH] * (3 * len(B_GROUPS))
               + [B_WIDTH]
               + [C_WIDTH] * 4
               + [N_BRANCH * D_MODEL])
N_IN = int(sum(SPLIT_SIZES))
SPLIT_POINTS = [int(v) for v in np.cumsum(SPLIT_SIZES)[:-1]]

kernel_name = "hybrid_diffattn_dilated_shortconv_gated_merge"

def _rmsnorm(x, g):
    xf = x.astype(jnp.float32)
    y = xf * lax.rsqrt(jnp.mean(xf * xf, axis=-1, keepdims=True) + RMS_EPS)
    return (y * g.astype(jnp.float32)).astype(x.dtype)

def _alibi_slopes(n):
    return jnp.asarray(2.0 ** (-8.0 * np.arange(1, n + 1) / n), dtype=jnp.float32)

def _diff_attention(q, k, v, lam, slopes):
    bsz, seq = q.shape[:2]
    nb = seq // Q_BLOCK
    q = q.reshape(bsz, nb, Q_BLOCK, A_HEADS, 2, A_HEAD_DIM).transpose(1, 0, 2, 3, 4, 5)
    k = k.reshape(bsz, seq, A_HEADS, 2, A_HEAD_DIM)
    v = v.reshape(bsz, seq, A_HEADS, 2 * A_HEAD_DIM)
    kpos = jnp.arange(seq)
    scale = A_HEAD_DIM ** -0.5

    def one_block(args):
        qb, i = args
        s = jnp.einsum('bqhmd,bkhmd->bhmqk', qb, k, preferred_element_type=jnp.float32) * scale
        dist = (i * Q_BLOCK + jnp.arange(Q_BLOCK))[:, None] - kpos[None, :]
        s = s - slopes[:, None, None, None] * dist.astype(jnp.float32)
        s = jnp.where(dist >= 0, s, -jnp.inf)
        p = jax.nn.softmax(s, axis=-1)
        p = p[:, :, 0] - lam * p[:, :, 1]
        return jnp.einsum('bhqk,bkhe->bqhe', p.astype(v.dtype), v)

    o = lax.map(one_block, (q, jnp.arange(nb)))
    return o.transpose(1, 0, 2, 3, 4).reshape(bsz, seq, A_HEADS, 2 * A_HEAD_DIM)

def _dilated_group(q, k, v, dilation, n_offsets, slopes):
    bsz, seq, nh, hd = q.shape
    sub = seq // dilation
    nb = -(-sub // Q_BLOCK)
    subp = nb * Q_BLOCK

    def to_sub(t):
        t = t.reshape(bsz, sub, dilation, nh, hd).transpose(0, 2, 1, 3, 4)
        return jnp.pad(t, ((0, 0), (0, 0), (0, subp - sub), (0, 0), (0, 0)))

    def band(t):
        t = jnp.pad(to_sub(t), ((0, 0), (0, 0), (Q_BLOCK, 0), (0, 0), (0, 0)))
        t = t.reshape(bsz, dilation, nb + 1, Q_BLOCK, nh, hd)
        return jnp.concatenate([t[:, :, :-1], t[:, :, 1:]], axis=3)

    qs = to_sub(q).reshape(bsz, dilation, nb, Q_BLOCK, nh, hd)
    kb, vb = band(k), band(v)
    s = jnp.einsum('brnqhd,brnkhd->brnhqk', qs, kb,
                   preferred_element_type=jnp.float32) * (hd ** -0.5)
    qi = jnp.arange(Q_BLOCK)[:, None]
    ki = jnp.arange(2 * Q_BLOCK)[None, :]
    off = Q_BLOCK + qi - ki
    key_idx = (jnp.arange(nb)[:, None, None] - 1) * Q_BLOCK + ki
    valid = (off >= 0) & (off <= n_offsets) & (key_idx >= 0)
    s = s - slopes[:, None, None] * (off * dilation).astype(jnp.float32)
    s = jnp.where(valid[:, None], s, -jnp.inf)
    lse = jax.nn.logsumexp(s, axis=-1, keepdims=True)
    p = jnp.exp(s - lse)
    o = jnp.einsum('brnhqk,brnkhd->brnqhd', p.astype(v.dtype), vb)
    o = o.reshape(bsz, dilation, subp, nh, hd)[:, :, :sub]
    o = o.transpose(0, 2, 1, 3, 4).reshape(bsz, seq, nh, hd)
    lse = lse[..., 0].transpose(0, 1, 2, 4, 3).reshape(bsz, dilation, subp, nh)[:, :, :sub]
    lse = lse.transpose(0, 2, 1, 3).reshape(bsz, seq, nh)
    return o, lse

def setup_inputs(seed: int = 0) -> dict:
    key = jax.random.key(seed)
    ks = jax.random.split(key, 16)
    f32 = jnp.float32
    nrm = lambda k, shape, s: (jax.random.normal(k, shape, f32) * s).astype(f32)
    return {
        "x": nrm(ks[0], (BATCH, SEQ, D_MODEL), 1.0),
        "norm_g": 1.0 + nrm(ks[1], (DEPTH, D_MODEL), 0.02),
        "w_in": nrm(ks[2], (DEPTH, D_MODEL, N_IN), D_MODEL ** -0.5),
        "gate_b": nrm(ks[3], (DEPTH, N_BRANCH * D_MODEL), 0.02),
        "lambda_q1": nrm(ks[4], (DEPTH, A_HEAD_DIM), 0.1),
        "lambda_k1": nrm(ks[5], (DEPTH, A_HEAD_DIM), 0.1),
        "lambda_q2": nrm(ks[6], (DEPTH, A_HEAD_DIM), 0.1),
        "lambda_k2": nrm(ks[7], (DEPTH, A_HEAD_DIM), 0.1),
        "subln_g": 1.0 + nrm(ks[8], (DEPTH, 2 * A_HEAD_DIM), 0.02),
        "conv_w": nrm(ks[9], (DEPTH, C_CONV, C_WIDTH), C_CONV ** -0.5),
        "w_branch_a": nrm(ks[10], (DEPTH, A_WIDTH, D_MODEL), A_WIDTH ** -0.5),
        "w_branch_b": nrm(ks[11], (DEPTH, B_WIDTH, D_MODEL), B_WIDTH ** -0.5),
        "w_branch_c": nrm(ks[12], (DEPTH, C_WIDTH, D_MODEL), C_WIDTH ** -0.5),
        "w_out": nrm(ks[13], (DEPTH, D_MODEL, D_MODEL), D_MODEL ** -0.5),
        "final_g": 1.0 + nrm(ks[14], (D_MODEL,), 0.02),
    }

def reference(x, norm_g, w_in, gate_b, lambda_q1, lambda_k1, lambda_q2, lambda_k2,
              subln_g, conv_w, w_branch_a, w_branch_b, w_branch_c, w_out, final_g):
    bsz, seq, _ = x.shape
    slopes = _alibi_slopes(N_ALIBI)
    slopes_a = slopes[:A_HEADS]
    n_g = len(B_GROUPS)
    for l in range(DEPTH):
        h = _rmsnorm(x, norm_g[l])
        proj = jnp.einsum('bsd,df->bsf', h, w_in[l])
        parts = jnp.split(proj, SPLIT_POINTS, axis=-1)
        aq, ak, av, az = parts[0:4]
        b_qkv = parts[4:4 + 3 * n_g]
        bz = parts[4 + 3 * n_g]
        cb, cc, cx, cz = parts[5 + 3 * n_g:9 + 3 * n_g]
        gates = jax.nn.sigmoid(parts[9 + 3 * n_g] + gate_b[l]).reshape(bsz, seq, N_BRANCH, D_MODEL)

        lam_init = 0.8 - 0.6 * math.exp(-0.3 * l)
        lam = (jnp.exp(jnp.sum(lambda_q1[l] * lambda_k1[l]).astype(jnp.float32))
               - jnp.exp(jnp.sum(lambda_q2[l] * lambda_k2[l]).astype(jnp.float32)) + lam_init)
        oa = _diff_attention(aq, ak, av, lam, slopes_a)
        oa = (_rmsnorm(oa, subln_g[l]) * (1.0 - lam_init)).reshape(bsz, seq, A_WIDTH)
        ya = oa * jax.nn.silu(az)

        outs, lses = [], []
        for g, (window, dil) in enumerate(B_GROUPS):
            q, k, v = [t.reshape(bsz, seq, B_HEADS, B_HEAD_DIM) for t in b_qkv[3 * g:3 * g + 3]]
            o, lse = _dilated_group(q, k, v, dil, window // dil,
                                    slopes[A_HEADS + g * B_HEADS:A_HEADS + (g + 1) * B_HEADS])
            outs.append(o)
            lses.append(lse)
        wgt = jax.nn.softmax(jnp.stack(lses, axis=0), axis=0)
        ob = jnp.sum(wgt[..., None].astype(x.dtype) * jnp.stack(outs, axis=0), axis=0)
        yb = ob.reshape(bsz, seq, B_WIDTH) * jax.nn.silu(bz)

        u = jnp.pad(cc * cx, ((0, 0), (C_CONV - 1, 0), (0, 0)))
        conv = sum(conv_w[l][j] * u[:, j:j + seq] for j in range(C_CONV))
        yc = cb * conv * jax.nn.silu(cz)

        merged = (gates[:, :, 0] * jnp.einsum('bsw,wd->bsd', ya, w_branch_a[l])
                  + gates[:, :, 1] * jnp.einsum('bsw,wd->bsd', yb, w_branch_b[l])
                  + gates[:, :, 2] * jnp.einsum('bsw,wd->bsd', yc, w_branch_c[l]))
        x = x + jnp.einsum('bsd,de->bse', merged, w_out[l])
    return _rmsnorm(x, final_g)


_drawn_inputs = setup_inputs


def setup_inputs(seed=0):
    import zlib

    import numpy as np

    out = dict(_drawn_inputs(seed))
    spreads = {}
    factors = {'norm_g': 3.526,
     'gate_b': 8.0,
     'lambda_q1': 2.884,
     'lambda_k1': 7.938,
     'lambda_q2': 8.0,
     'lambda_k2': 3.275,
     'subln_g': 8.0,
     'final_g': 2.784}
    for name, (base, spread) in spreads.items():
        noise = np.random.default_rng([zlib.crc32(name.encode()), seed]).standard_normal(out[name].shape)
        drawn = base * np.exp(spread * noise) if base else spread * noise
        out[name] = __import__('jax').numpy.asarray(drawn.astype(out[name].dtype))
    for name, factor in factors.items():
        out[name] = (out[name] * factor).astype(out[name].dtype)
    return out
```

```python
import math
from contextlib import ExitStack

import concourse.bass as bass
from concourse import mybir

P = 128
D = 2048
T = 512
KT = D // P
HEADS = 8
HU = 8 * P
RING = 3
NBLK1, NBLK2, NBLK3 = 18, 6, 16
NHU1, NHU2 = 36, 9
W1 = HEADS * NHU1
W2 = KT * NHU2
W3 = 2 * NBLK3
LAM_INIT = 0.8 - 0.6 * math.exp(-0.3 * 0)
EPS = 1e-6
FAR = 1e30
SCALE_A = 64 ** -0.5
SCALE_B = 128 ** -0.5
C_MA, C_M0, C_M12, C_ID, C_ONE, C_SL = 0, 512, 512 + 515, 1283, 1283 + 128, 1283 + 256
C_END = C_SL + 4 * HEADS
S_G, S_GB, S_SUB, S_CONV, S_FG = 0, 16, 64, 65, 89
S_END = 105
Y_ITEMS = [1, 2, 2, 2, 2, 2, 1, 0, 0]
N_Y, N_M = 12, 8
AQ, AK, AV, AZ, Q0, K0, Q1, K1, Q2, K2, V0, V1, V2, BZ, CB, CC, CX, CZ = range(NBLK1)


def ring_index(n):
    return n + N_Y + (N_M if n >= W1 + W2 + RING else 0)


def first_merged_ring():
    ticks, y = [], 0
    for t in range(NHU2):
        items = [("y", y + m) for m in range(Y_ITEMS[t])]
        y += Y_ITEMS[t]
        ticks.append(items + [("w", W1 + RING + t)])
    return ticks


def program(nc, wst, x_t, cols_d, lam_d, const_d, out_d):
    f32, f32r = mybir.dt.float32, mybir.dt.float32r
    ALU, ACT, AX = mybir.AluOpType, mybir.ActivationFunctionType, mybir.AxisListType
    y_dram = nc.dram_tensor("y_dram", (3 * HEADS, P, T), f32, kind="Internal").ap()
    m_dram = nc.dram_tensor("m_dram", (KT, P, T), f32, kind="Internal").ap()

    with ExitStack() as ctx:
        def sb_in(c):
            return lambda name, shape, dt=f32: c.enter_context(nc.sbuf_tensor(name, shape, dt))

        def sem(name):
            return ctx.enter_context(nc.semaphore(name))

        sb = sb_in(ctx)
        act_hi, act_lo = sb("act_hi", [P, KT, T], f32r), sb("act_lo", [P, KT, T], f32r)
        raw = [sb(f"raw{i}", [P, HU]) for i in range(RING)]
        w_hi = [sb(f"w_hi{i}", [P, HU], f32r) for i in range(RING)]
        w_lo = [sb(f"w_lo{i}", [P, HU], f32r) for i in range(RING)]
        rstd = sb("rstd", [P, T])
        cols = sb("cols", [P, S_END])
        eps = sb("eps", [P, 1])
        lam_col = sb("lam_col", [P, 1])
        gsub = sb("gsub", [P, 1])
        ones = sb("ones", [P, P])

        with ExitStack() as c1:
            s1 = sb_in(c1)
            masks = s1("masks", [P, C_ID])
            ident = s1("ident", [P, P])
            slopes = s1("slopes", [P, 4 * HEADS])
            slope = s1("slope", [P, 4])
            taps = s1("taps", [P, 3])
            lam_in = s1("lam_in", [1, 4 * 64])
            lam_w = s1("lam_w", [1, 2 * 64])
            lam_s = s1("lam_s", [1, 8])
            blk = {b: s1(f"blk{b}", [P, T]) for b in (AQ, AK, AV, AZ, Q0, K0, Q1, K1, Q2, K2, V0, V1, BZ, CB, CC, CX)}
            blk[V2], blk[CZ] = blk[AV], blk[AZ]
            th = s1("th", [P, T])
            sc_a, p_a, tmp_a = s1("sc_a", [P, 2, T]), s1("p_a", [P, T]), s1("tmp_a", [P, T])
            v_a, pt_a = s1("v_a", [P, 4, P]), s1("pt_a", [P, 4, T])
            o_a, sq_a, inv_a, y_a = s1("o_a", [P, T]), s1("sq_a", [P, T]), s1("inv_a", [P, T]), s1("y_a", [P, T])
            nmax, sums, rsum = s1("nmax", [P, 2]), s1("sums", [P, 2]), s1("rsum", [P, 2])
            sc_b, p_b = s1("sc_b", [P, 6 * P]), s1("p_b", [P, 6 * P])
            v_b = [s1(f"v_b{g}", [P, 4, P]) for g in range(3)]
            pt_b = s1("pt_b", [P, 6, 4, P])
            y_b = s1("y_b", [P, T])
            u = s1("u", [P, T + 2])
            y_c = s1("y_c", [P, T])
        with ExitStack() as c0:
            s0 = sb_in(c0)
            s0("below", [P, C_ID + P + 8 * HEADS + 1024])
            x_raw = s0("x_raw", [P, KT, T])
            xg = [s0(f"xg{i}", [P, T]) for i in range(2)]
            xsq = [s0(f"xsq{i}", [P, T]) for i in range(2)]
        with ExitStack() as c2:
            s2 = sb_in(c2)
            gate = [s2(f"gate{b}", [P, T]) for b in range(3)]
            merged = s2("merged", [P, T])
            y_hi, y_lo = s2("y_hi", [P, 3 * HEADS, T], f32r), s2("y_lo", [P, 3 * HEADS, T], f32r)
        with ExitStack() as c3:
            s3 = sb_in(c3)
            res = s3("res", [P, KT, T])
            rsq = [s3(f"rsq{i}", [P, T]) for i in range(RING)]
            frstd = s3("frstd", [P, T])
            fin = [s3(f"fin{i}", [P, T]) for i in range(4)]

        pb = [ctx.enter_context(nc.psum_tensor(f"proj{i}", [P, T], f32)) for i in range(RING)]
        sc_ps = [ctx.enter_context(nc.psum_tensor(f"sc_ps{i}", [P, T], f32)) for i in range(2)]
        tr_ps = [ctx.enter_context(nc.psum_tensor(f"tr_ps{i}", [P, T], f32)) for i in range(2)]
        o_ps = ctx.enter_context(nc.psum_tensor("o_ps", [P, T], f32))

        const_in = sem("const_in")
        x_in = [sem(f"x_in{i}") for i in range(8)]
        res_in = sem("res_in")
        raw_in = [sem(f"raw_in{i}") for i in range(RING)]
        y_stored = [sem(f"y_stored{b}") for b in range(3)]
        m_stored = sem("m_stored")
        out_stored = [sem(f"out_stored{i}") for i in range(4)]
        hi_done, lo_done, pe_used = sem("hi_done"), sem("lo_done"), sem("pe_used")
        evac_done = sem("evac_done")
        xg_done, xh_done, xl_done = sem("xg_done"), sem("xh_done"), sem("xl_done")
        xsq_done, xsq_used, std_done = sem("xsq_done"), sem("xsq_used"), sem("std_done")
        lam_sum, lam_exp, lam_set, lam_bc = sem("lam_sum"), sem("lam_exp"), sem("lam_set"), sem("lam_bc")
        s_ready, s_free = sem("s_ready"), sem("s_free")
        t_ready, t_free = sem("t_ready"), sem("t_free")
        o_ready, o_free = sem("o_ready"), sem("o_free")
        biased, exp_done, p_ready = sem("biased"), sem("exp_done"), sem("p_ready")
        th_ready, sq_ready, sd_ready, y_ready = sem("th_ready"), sem("sq_ready"), sem("sd_ready"), sem("y_ready")
        gate_done, m_ready = sem("gate_done"), sem("m_ready")
        rsq_done, fin_ready = sem("rsq_done"), sem("fin_ready")
        dve_step = sem("dve_step")

        block = ctx.enter_context(nc.Block())

        def natural(ap):
            return ap

        def by_class(ap):
            return ap.rearrange("p (b c) -> p c b", c=4)

        def as_class(ap):
            return ap.rearrange("p (c b) -> p c b", c=4)

        @block.sync
        def _(sp):
            def load_w(slot, n):
                src = wst[n, :, :] if isinstance(n, int) else wst[bass.ds(n, 1), :, :].rearrange("o p f -> p (o f)")
                sp.dma_start(raw[slot][:, :], src).then_inc(raw_in[slot], 16)

            def load_pair(slot, dram, item):
                sp.dma_start(raw[slot][:, :].rearrange("p (t q) -> p t q", t=2),
                             dram[2 * item:2 * item + 2, :, :].rearrange("t p q -> p t q")).then_inc(raw_in[slot], 16)

            for r in range(RING):
                load_w(r, r)
            with sp.Fori(1, W1 // RING + 1) as i:
                for s in range(RING):
                    sp.wait_ge(lo_done, RING * i + s - RING + 1)
                    load_w(s, RING * i + s)
            for b in range(3):
                sp.wait_ge(y_stored[b], 16 * (HEADS + 1))
            r = W1 + RING
            for kind, n in [x for tick in first_merged_ring() for x in tick]:
                sp.wait_ge(lo_done, r - RING + 1)
                if kind == "y":
                    load_pair(r % RING, y_dram, n)
                else:
                    load_w(r % RING, n)
                r += 1
            n0 = W1 + NHU2 + RING
            with sp.Fori(0, (KT - 1) * NHU2 // RING) as i:
                for s in range(RING):
                    sp.wait_ge(lo_done, RING * i + (r + s - RING + 1))
                    load_w((r + s) % RING, RING * i + (n0 + s))
            r += (KT - 1) * NHU2
            sp.wait_ge(m_stored, 16 * (KT + 1))
            for item in range(N_M):
                sp.wait_ge(lo_done, r - RING + 1)
                load_pair(r % RING, m_dram, item)
                r += 1
            n0 = W1 + W2 + RING
            left = W3 - RING
            with sp.Fori(0, left // RING) as i:
                for s in range(RING):
                    sp.wait_ge(lo_done, RING * i + (r + s - RING + 1))
                    load_w((r + s) % RING, RING * i + (n0 + s))
            for s in range(left - left % RING, left):
                sp.wait_ge(lo_done, r + s - RING + 1)
                load_w((r + s) % RING, n0 + s)

        @block.tensor
        def _(pe):
            pe.sem_inc(pe_used, RING)
            pe.wait_ge(const_in, 16 * 6)

            def multiply(bank, slot, m_hi, m_lo, k0, first, last):
                for k in range(8):
                    ws = slice(k * P, (k + 1) * P)
                    a, b = m_hi[:, k0 + k, :], m_lo[:, k0 + k, :]
                    nc.tensor.matmul(pb[bank][:, :], w_hi[slot][:, ws], a, start=first and k == 0, stop=False)
                    nc.tensor.matmul(pb[bank][:, :], w_hi[slot][:, ws], b, start=False, stop=False)
                    end = nc.tensor.matmul(pb[bank][:, :], w_lo[slot][:, ws], a, start=False, stop=last and k == 7)
                end.then_inc(pe_used, 1)

            for k in range(KT):
                pe.wait_ge(xsq_done, k + 1)
                nc.tensor.matmul(o_ps[:, :], ones[:, :], xsq[k % 2][:, :], start=k == 0,
                                 stop=k == KT - 1).then_inc(xsq_used, 1)
            pe.wait_ge(lam_set, 1)
            nc.tensor.matmul(tr_ps[0][:, 0:1], ones[0:1, :], lam_s[0:1, 4:5], start=True, stop=True).then_inc(lam_bc, 1)
            pe.wait_ge(xl_done, KT)

            def scaled(i, b):
                pe.wait_ge(evac_done, NBLK1 * i + (RING + b + 1))

            def scores_a(i, q):
                n = P * (q + 1)
                scaled(i, AK)
                pe.wait_ge(s_free, 9 * i + (q + 1))
                for m in range(2):
                    rows = slice(64 * m, 64 * m + 64)
                    end = nc.tensor.matmul(sc_ps[m][:, 0:n], blk[AQ][rows, P * q:P * q + P], blk[AK][rows, 0:n],
                                           start=True, stop=True)
                end.then_inc(s_ready, 1)

            def turn(i, idx, tiles):
                pe.wait_ge(t_free, 16 * i + (idx + 1))
                for n, tile in enumerate(tiles):
                    end = nc.tensor.transpose(tr_ps[idx % 2][:, n * P:(n + 1) * P], tile, ident[:, :])
                end.then_inc(t_ready, 1)

            def probs_a(i, q):
                pe.wait_ge(p_ready, 8 * i + (q + 1))
                turn(i, 1 + q, [p_a[:, n * P:(n + 1) * P] for n in range(q + 1)])

            def values_a(i):
                pe.wait_ge(t_free, 16 * i + (2 + 5))
                pe.wait_ge(o_free, 2 * i + 1)
                for n in range(4):
                    end = nc.tensor.matmul(o_ps[:, n * P:T], v_a[:, n, :], pt_a[:, n, n * P:T], start=n == 0, stop=n == 3)
                end.then_inc(o_ready, 1)

            def squares_a(i):
                pe.wait_ge(sq_ready, i + 1)
                pe.wait_ge(s_free, 9 * i + 5)
                nc.tensor.matmul(sc_ps[0][:, :], ones[:, :], sq_a[:, :], start=True, stop=True).then_inc(s_ready, 1)

            def scores_b(i, c):
                scaled(i, K2)
                pe.wait_ge(s_free, 9 * i + (6 + c))
                qs = slice(c * P, (c + 1) * P)
                nc.tensor.matmul(sc_ps[0][:, :], blk[Q0][:, qs], blk[K0][:, :], start=True, stop=True)
                nc.tensor.matmul(sc_ps[1][:, 0:P], blk[Q1][:, qs], blk[K1][:, qs], start=True, stop=True)
                nc.tensor.matmul(sc_ps[1][:, P:2 * P], blk[Q2][:, qs], blk[K2][:, qs], start=True, stop=True).then_inc(s_ready, 1)

            first_turn = [5, 8, 11, 14]

            def probs_b(i, c):
                pe.wait_ge(p_ready, 8 * i + (5 + c))
                turn(i, first_turn[c], [p_b[:, n * P:(n + 1) * P] for n in range(4)])
                turn(i, first_turn[c] + 1, [p_b[:, n * P:(n + 1) * P] for n in range(4, 6)])

            def values_b(i):
                pe.wait_ge(t_free, 16 * i + (2 + 16))
                pe.wait_ge(o_free, 2 * i + 2)
                for n in range(4):
                    nc.tensor.matmul(o_ps[:, :], v_b[0][:, n, :], pt_b[:, n, :, :], start=n == 0, stop=False)
                for g in (1, 2):
                    for c in range(4):
                        end = nc.tensor.matmul(o_ps[:, c * P:(c + 1) * P], v_b[g][:, c, :], pt_b[:, 3 + g, c, :],
                                               start=False, stop=g == 2 and c == 3)
                end.then_inc(o_ready, 1)

            def quarter(tile):
                return [tile[:, n * P:(n + 1) * P] for n in range(4)]

            with pe.Fori(0, HEADS) as i:
                for w in range(NBLK1):
                    pe.wait_ge(evac_done, NBLK1 * i + (w + 1))
                    pe.wait_ge(lo_done, NHU1 * i + (2 * w + 1))
                    multiply(w % RING, 2 * w % RING, act_hi, act_lo, 0, True, False)
                    if w == 12:
                        scaled(i, V0)
                        turn(i, 7, quarter(blk[V0]))
                    if w == 13:
                        scaled(i, V1)
                        turn(i, 10, quarter(blk[V1]))
                    if w == 14:
                        scaled(i, V2)
                        turn(i, 13, quarter(blk[V2]))
                    pe.wait_ge(lo_done, NHU1 * i + (2 * w + 2))
                    multiply(w % RING, (2 * w + 1) % RING, act_hi, act_lo, 8, False, True)
                    if 2 <= w < 6:
                        scores_a(i, w - 2)
                    if w == 3:
                        scaled(i, AV)
                        turn(i, 0, quarter(blk[AV]))
                    if 3 <= w < 7:
                        probs_a(i, w - 3)
                    if w == 7:
                        values_a(i)
                    if w == 8:
                        squares_a(i)
                    if 10 <= w < 14:
                        scores_b(i, w - 10)
                    if 11 <= w < 15:
                        probs_b(i, w - 11)
                    if w == 15:
                        values_b(i)

            def merge_block(evac, ready, y_needed=(0, 0, 0)):
                for b in range(3):
                    pe.wait_ge(evac_done, evac + (b + 1))
                    for half in range(2):
                        pe.wait_ge(lo_done, ready[2 * b + half])
                        multiply(b, (2 * b + half) % RING, act_hi, act_lo, 8 * half, half == 0, half == 1)
                for b in range(3):
                    pe.wait_ge(evac_done, evac + (b + 4))
                    pe.wait_ge(lo_done, ready[6 + b])
                    if y_needed[b]:
                        pe.wait_ge(lo_done, y_needed[b])
                    multiply(b, (6 + b) % RING, y_hi, y_lo, 8 * b, True, True)

            place = {x: W1 + RING + m for m, x in enumerate(x for tick in first_merged_ring() for x in tick)}
            evac0 = NBLK1 * HEADS
            merge_block(evac0, [W1 + t + 1 if t < RING else place[("w", W1 + t)] + 1 for t in range(NHU2)],
                        [place[("y", 4 * b + 3)] + 1 for b in range(3)])
            with pe.Fori(1, KT) as j:
                merge_block(NBLK2 * j + evac0, [NHU2 * j + (W1 + N_Y + t + 1) for t in range(NHU2)])

            evac0 += NBLK2 * KT
            n0 = W1 + W2

            def out_block(bank, slot, evac, ready):
                pe.wait_ge(evac_done, evac + 1)
                for half in range(2):
                    pe.wait_ge(lo_done, ready[half])
                    multiply(bank, (slot + half) % RING, act_hi, act_lo, 8 * half, half == 0, half == 1)

            def out_squares(done, slot, first, last):
                pe.wait_ge(rsq_done, done)
                nc.tensor.matmul(o_ps[:, :], ones[:, :], rsq[slot][:, :], start=first, stop=last,
                                 skip_group_check=True).then_inc(xsq_used, 1)

            pe.wait_ge(lo_done, W1 + W2 + RING + N_Y + N_M)
            out_block(0, 0, evac0, [n0 + N_Y + 1, n0 + N_Y + 2])
            n1, r1 = n0 + 2, n0 + 2 + N_Y + N_M

            def out_round(m, first):
                for s in range(3):
                    ready = [6 * m + (r1 + 2 * s + half + 1) for half in range(2)]
                    if first and s == 0:
                        ready[0] = n0 + 2 + N_Y + 1
                    out_block((1 + s) % RING, (2 + 2 * s) % RING, 3 * m + (evac0 + 1 + s), ready)
                    out_squares(3 * m + (s + 1), s, first and s == 0, False)

            out_round(0, True)
            with pe.Fori(1, 5) as m:
                out_round(m, False)
            out_squares(NBLK3, (NBLK3 - 1) % RING, False, True)

        @block.scalar
        def _(act):
            for g in range(8):
                act.dma_start(x_raw[:, 2 * g:2 * g + 2, :], x_t[2 * g:2 * g + 2, :, :].rearrange("k p t -> p k t")).then_inc(x_in[g], 16)
                if g == 0:
                    act.dma_start(cols[:, :], cols_d).then_inc(const_in, 16)
                    act.dma_start(lam_in[:, :], lam_d).then_inc(const_in, 16)
                    act.dma_start(ones[:, :], const_d[:, C_ONE:C_ONE + P]).then_inc(const_in, 16)
            act.dma_start(masks[:, :], const_d[:, 0:C_ID]).then_inc(const_in, 16)
            act.dma_start(ident[:, :], const_d[:, C_ID:C_ID + P]).then_inc(const_in, 16)
            act.dma_start(slopes[:, :], const_d[:, C_SL:C_END]).then_inc(const_in, 16)
            act.sem_inc(t_free, 2)
            for b in range(3):
                act.sem_inc(y_stored[b], 16)
            act.sem_inc(m_stored, 16)

            def loaded(slot, r):
                if isinstance(r, int):
                    act.wait_ge(raw_in[slot], 16 * (r // RING + 1))

            def split_hi(slot_raw, slot_w, used, loads):
                act.wait_ge(raw_in[slot_raw], 16 * loads)
                act.wait_ge(pe_used, used)
                nc.scalar.activation(w_hi[slot_w][:, :], raw[slot_raw][:, :], ACT.Copy).then_inc(hi_done, 1)

            def split_hi_pair(slot_raw, dst, item, loads):
                act.wait_ge(raw_in[slot_raw], 16 * loads)
                nc.scalar.activation(dst[:, 2 * item:2 * item + 2, :].rearrange("p t q -> p (t q)"),
                                     raw[slot_raw][:, :], ACT.Copy).then_inc(hi_done, 1)

            act.wait_ge(const_in, 16 * 6)
            for k in range(KT):
                act.wait_ge(x_in[k // 2], 16)
                if k >= 2:
                    act.wait_ge(xsq_used, k - 1)
                nc.scalar.activation(xsq[k % 2][:, :], x_raw[:, k, :], ACT.Square).then_inc(xsq_done, 1)
                act.wait_ge(xg_done, k + 1)
                nc.scalar.activation(act_hi[:, k, :], xg[k % 2][:, :], ACT.Copy).then_inc(xh_done, 1)
                if k in (4, 8, 12):
                    n = k // 4 - 1
                    split_hi(n, n, n + 1, 1)
                if k == 2:
                    act.wait_ge(lam_sum, 1)
                    nc.scalar.activation(lam_s[0:1, 2:4], lam_s[0:1, 0:2], ACT.Exp).then_inc(lam_exp, 1)
            act.wait_ge(xsq_used, KT)
            nc.scalar.activation(rstd[:, :], o_ps[:, :], ACT.Sqrt, scale=1.0 / D, bias=eps[:, :]).then_inc(std_done, 1)

            def split_1(i, t):
                split_hi(t % RING, t % RING, NHU1 * i + (t + RING + 1), (NHU1 // RING) * i + (t // RING + 2))

            def exps(i, idx, tile, spans, scale):
                act.wait_ge(biased, 8 * i + (idx + 1))
                for m, (lo, hi) in enumerate(spans):
                    end = nc.scalar.activation(tile[:, lo:hi], tile[:, lo:hi], ACT.Exp, scale=scale,
                                               bias=nmax[:, m:m + 1], accum_out=sums[:, m:m + 1])
                end.then_inc(exp_done, 1)

            def turned(i, idx, dst, n):
                act.wait_ge(t_ready, 16 * i + (idx + 1))
                nc.scalar.activation(dst, tr_ps[idx % 2][:, 0:n * P].rearrange("p (n q) -> p n q", n=n),
                                     ACT.Copy).then_inc(t_free, 1)

            def tanh_half(i, w):
                act.wait_ge(evac_done, NBLK1 * i + (RING + w + 1))
                nc.scalar.activation(th[:, :], blk[w][:, :], ACT.Tanh, scale=0.5).then_inc(th_ready, 1)

            def store_y(i, b, tile):
                act.dma_start(y_dram[bass.ds(i + HEADS * b, 1), :, :].rearrange("o p q -> p (o q)"), tile[:, :]).then_inc(y_stored[b], 16)

            first_turn = [5, 8, 11, 14]
            sc_flat = sc_a[:, :, :].rearrange("p m q -> p (m q)")
            with act.Fori(0, HEADS) as i:
                for w in range(NBLK1):
                    split_1(i, 2 * w)
                    if 12 <= w < 15:
                        turned(i, first_turn[w - 12] + 2, v_b[w - 12][:, :, :], 4)
                    split_1(i, 2 * w + 1)
                    if w == 3:
                        turned(i, 0, v_a[:, :, :], 4)
                    if 3 <= w < 7:
                        q = w - 3
                        turned(i, 1 + q, pt_a[:, 0:q + 1, q * P:(q + 1) * P], q + 1)
                    if 11 <= w < 15:
                        c = w - 11
                        turned(i, first_turn[c], pt_b[:, 0:4, c, :], 4)
                        turned(i, first_turn[c] + 1, pt_b[:, 4:6, c, :], 2)
                    if 2 <= w < 6:
                        q = w - 2
                        exps(i, q, sc_flat, [(m * T, m * T + P * (q + 1)) for m in range(2)], SCALE_A)
                    if 10 <= w < 14:
                        exps(i, 4 + w - 10, sc_b, [(0, 6 * P)], SCALE_B)
                    if w in (AZ, BZ, CZ):
                        tanh_half(i, w)
                    if w == 7:
                        act.wait_ge(o_free, 2 * i + 2)
                        nc.scalar.activation(sq_a[:, :], o_a[:, :], ACT.Square).then_inc(sq_ready, 1)
                    if w == 8:
                        act.wait_ge(s_free, 9 * i + 6)
                        nc.scalar.activation(inv_a[:, :], sq_a[:, :], ACT.Sqrt).then_inc(sd_ready, 1)
                    if w == 9:
                        act.wait_ge(y_ready, 2 * i + 1)
                        store_y(i, 0, y_a)
                    if w == 15:
                        act.wait_ge(o_free, 2 * i + 3)
                        store_y(i, 1, y_b)
                    if w == CZ:
                        act.wait_ge(y_ready, 2 * i + 2)
                        store_y(i, 2, y_c)

            def tanh_gate(done, b, col):
                act.wait_ge(evac_done, done)
                nc.scalar.activation(gate[b][:, :], gate[b][:, :], ACT.Tanh, scale=0.5, bias=col).then_inc(gate_done, 1)

            evac0 = NBLK1 * HEADS + RING

            r = W1 + RING
            for t, tick in enumerate(first_merged_ring()):
                for kind, n in tick:
                    if kind == "y":
                        split_hi_pair(r % RING, y_hi, n, r // RING + 1)
                    else:
                        split_hi(r % RING, n % RING, n + 1, r // RING + 1)
                    r += 1
                if t in (1, 3, 5):
                    b = t // 2
                    tanh_gate(evac0 + b + 1, b, cols[:, S_GB + b:S_GB + b + 1])
            act.wait_ge(m_ready, 1)
            act.dma_start(m_dram[0, :, :], merged[:, :]).then_inc(m_stored, 16)
            with act.Fori(1, KT) as j:
                for t in range(NHU2):
                    split_hi(t % RING, t % RING, NHU2 * j + (W1 + RING + t + 1),
                             (NHU2 // RING) * j + ((W1 + N_Y + RING + t) // RING + 1))
                    if t in (1, 3, 5):
                        b = t // 2
                        tanh_gate(NBLK2 * j + (evac0 + b + 1), b, cols[:, bass.ds(3 * j + (S_GB + b), 1)])
                act.wait_ge(m_ready, j + 1)
                act.dma_start(m_dram[bass.ds(j, 1), :, :].rearrange("o p q -> p (o q)"), merged[:, :]).then_inc(m_stored, 16)
            act.wait_ge(m_stored, 16 * (KT + 1))
            act.wait_ge(pe_used, W1 + W2 + RING)
            act.dma_start(res[:, :, :], x_t.rearrange("k p t -> p k t")).then_inc(res_in, 16)
            r = W1 + W2 + RING + N_Y
            for item in range(N_M):
                split_hi_pair((r + item) % RING, act_hi, item, (r + item) // RING + 1)
            r += N_M
            n = W1 + W2 + RING

            def split_3(m, t):
                a, b = r + 2 + t, n + 2 + t
                split_hi(a % RING, b % RING, 6 * m + (b + 1), 2 * m + (a // RING + 1))

            def square_out(evac, blk_i, s):
                act.wait_ge(evac_done, evac)
                src = res[:, blk_i, :] if isinstance(blk_i, int) else res[:, bass.ds(blk_i, 1), :].rearrange("p o q -> p (o q)")
                nc.scalar.activation(rsq[s][:, :], src, ACT.Square).then_inc(rsq_done, 1)

            evac1 = NBLK1 * HEADS + NBLK2 * KT + RING
            for t in range(2):
                a, b = r + t, n + t
                split_hi(a % RING, b % RING, b + 1, a // RING + 1)
            square_out(evac1 + 1, 0, 0)

            def out_round(m, splits):
                for s in range(3):
                    for half in range(2):
                        if 2 * s + half < splits:
                            split_3(m, 2 * s + half)
                    if not (isinstance(m, int) and m == 0 and s < 2):
                        act.wait_ge(xsq_used, 3 * m + (KT + s - 1))
                    square_out(3 * m + (evac1 + 2 + s), 3 * m + (1 + s), (1 + s) % RING)

            out_round(0, 6)
            with act.Fori(1, 4) as m:
                out_round(m, 6)
            out_round(4, 3)
            act.wait_ge(xsq_used, KT + NBLK3)
            nc.scalar.activation(frstd[:, :], o_ps[:, :], ACT.Sqrt, scale=1.0 / D, bias=eps[:, :]).then_inc(std_done, 1)
            for k in range(KT):
                act.wait_ge(fin_ready, k + 1)
                act.dma_start(out_d[k, :, :], fin[k % 4][:, :]).then_inc(out_stored[k % 4], 16)
            for s in range(4):
                act.wait_ge(out_stored[s], 16 * KT // 4)

        @block.vector
        def _(dve):
            steps = {"base": 0, "n": 0, "i": 0, "per": 0}

            def link(ins):
                steps["n"] += 1
                ins.then_inc(dve_step, 1)
                done = steps["base"] + steps["n"]
                dve.wait_ge(dve_step, steps["per"] * steps["i"] + done if steps["per"] else done)

            def enter(i, per):
                steps.update(i=i, per=per, base=steps["base"] + steps["n"], n=0)

            def leave(count):
                assert steps["n"] == steps["per"], steps
                steps.update(base=steps["base"] + steps["per"] * count, n=0, i=0, per=0)

            tt, ts, stt = nc.vector.tensor_tensor, nc.vector.tensor_scalar, nc.vector.scalar_tensor_tensor
            dve.sem_inc(evac_done, RING)
            dve.sem_inc(s_free, 1)
            dve.sem_inc(o_free, 1)
            nc.vector.memset(eps[:, :], EPS)
            nc.vector.memset(u[:, 0:2], 0.0)
            dve.wait_ge(const_in, 16 * 6)
            lam_v = lam_in[:, :].rearrange("o (a b d) -> o a b d", a=2, b=2)
            link(tt(lam_w[:, :].rearrange("o (a d) -> o a d", a=2), lam_v[:, :, 0, :], lam_v[:, :, 1, :], ALU.mult))
            nc.vector.reduce_sum(lam_s[:, 0:2], lam_w[:, :].rearrange("o (a d) -> o a d", a=2), AX.X).then_inc(lam_sum, 1)
            ts(gsub[:, :], cols[:, S_SUB:S_SUB + 1], 1.0 - LAM_INIT, None, ALU.mult)
            link(ts(cols[:, S_GB:S_GB + 48], cols[:, S_GB:S_GB + 48], 0.5, None, ALU.mult))

            def split_lo(slot_raw, slot_w, hi):
                dve.wait_ge(hi_done, hi)
                tt(w_lo[slot_w][:, :], raw[slot_raw][:, :], w_hi[slot_w][:, :].bitcast(f32), ALU.subtract).then_inc(lo_done, 1)

            def split_lo_pair(slot_raw, lo, hi_part, item, hi):
                dve.wait_ge(hi_done, hi)
                tt(lo[:, 2 * item:2 * item + 2, :].rearrange("p t q -> p (t q)"), raw[slot_raw][:, :],
                   hi_part[:, 2 * item:2 * item + 2, :].rearrange("p t q -> p (t q)").bitcast(f32), ALU.subtract).then_inc(lo_done, 1)

            def x_low(k):
                dve.wait_ge(xh_done, k + 1)
                tt(act_lo[:, k, :], xg[k % 2][:, :], act_hi[:, k, :].bitcast(f32), ALU.subtract).then_inc(xl_done, 1)

            for k in range(KT):
                dve.wait_ge(x_in[k // 2], 16)
                if k >= 2:
                    dve.wait_ge(xl_done, k - 1)
                ts(xg[k % 2][:, :], x_raw[:, k, :], cols[:, S_G + k:S_G + k + 1], None, ALU.mult).then_inc(xg_done, 1)
                if k >= 1:
                    x_low(k - 1)
                if k in (5, 9, 13):
                    n = k // 4 - 1
                    split_lo(n, n, n + 1)
                if k == 6:
                    dve.wait_ge(lam_exp, 1)
                    link(tt(lam_s[:, 6:7], lam_s[:, 2:3], lam_s[:, 3:4], ALU.subtract))
                    ts(lam_s[:, 4:5], lam_s[:, 6:7], LAM_INIT, None, ALU.add).then_inc(lam_set, 1)
            x_low(KT - 1)
            dve.wait_ge(lam_bc, 1)
            nc.vector.tensor_copy(lam_col[:, :], tr_ps[0][:, 0:1])
            dve.wait_ge(std_done, 1)
            link(nc.vector.reciprocal(rstd[:, :], rstd[:, :]))

            def split_1(i, t):
                split_lo(t % RING, t % RING, NHU1 * i + (t + RING + 1))

            classed = {Q0, Q1, K1, Q2, K2, V1, V2}

            def scale_block(i, w):
                dve.wait_ge(pe_used, NHU1 * i + (2 * w + 2 + RING))
                if w in classed:
                    ins = tt(as_class(blk[w][:, :]), by_class(pb[w % RING][:, :]), by_class(rstd[:, :]), ALU.mult)
                else:
                    ins = tt(blk[w][:, :], pb[w % RING][:, :], rstd[:, :], ALU.mult)
                ins.then_inc(evac_done, 1)

            def bias_a(i, q):
                n = P * (q + 1)
                dve.wait_ge(s_ready, 9 * i + (q + 1))
                if q:
                    dve.wait_ge(p_ready, 8 * i + q)
                for m in range(2):
                    end = stt(sc_a[:, m, 0:n], masks[:, C_MA + T - n:C_MA + T], slope[:, 0:1], sc_ps[m][:, 0:n], ALU.mult, ALU.add)
                end.then_inc(s_free, 1)
                dve.wait_ge(s_free, 9 * i + (q + 2))
                link(nc.vector.reduce_max(rsum[:, :], sc_a[:, :, 0:n], AX.X))
                ts(nmax[:, :], rsum[:, :], -SCALE_A, None, ALU.mult).then_inc(biased, 1)

            def norm_a(i, q):
                n = P * (q + 1)
                dve.wait_ge(exp_done, 8 * i + (q + 1))
                link(nc.vector.reciprocal(rsum[:, :], sums[:, :]))
                link(tt(rsum[:, 1:2], rsum[:, 1:2], lam_col[:, :], ALU.mult))
                link(ts(tmp_a[:, 0:n], sc_a[:, 1, 0:n], rsum[:, 1:2], None, ALU.mult))
                stt(p_a[:, 0:n], sc_a[:, 0, 0:n], rsum[:, 0:1], tmp_a[:, 0:n], ALU.mult, ALU.subtract).then_inc(p_ready, 1)

            def bias_b(i, c):
                dve.wait_ge(s_ready, 9 * i + (6 + c))
                if c:
                    dve.wait_ge(p_ready, 8 * i + (4 + c))
                m0 = C_M0 + 3 - c
                stt(sc_b[:, 0:T], masks[:, m0:m0 + T], slope[:, 1:2], sc_ps[0][:, :], ALU.mult, ALU.add)
                for g in (1, 2):
                    end = stt(sc_b[:, (3 + g) * P:(4 + g) * P], masks[:, C_M12 + (g - 1) * P:C_M12 + g * P],
                              slope[:, 1 + g:2 + g], sc_ps[1][:, (g - 1) * P:g * P], ALU.mult, ALU.add)
                end.then_inc(s_free, 1)
                dve.wait_ge(s_free, 9 * i + (7 + c))
                link(nc.vector.reduce_max(rsum[:, 0:1], sc_b[:, :], AX.X))
                ts(nmax[:, 0:1], rsum[:, 0:1], -SCALE_B, None, ALU.mult).then_inc(biased, 1)

            def norm_b(i, c):
                dve.wait_ge(exp_done, 8 * i + (5 + c))
                link(nc.vector.reciprocal(rsum[:, 0:1], sums[:, 0:1]))
                ts(p_b[:, :], sc_b[:, :], rsum[:, 0:1], None, ALU.mult).then_inc(p_ready, 1)

            def silu(i, idx, w):
                dve.wait_ge(th_ready, 3 * i + (idx + 1))
                link(stt(blk[w][:, :], th[:, :], 1.0, blk[w][:, :], ALU.add, ALU.mult))

            STEPS1 = 2 + 4 + 12 + 4 + 4 + 3 + 2 + 5
            with dve.Fori(0, HEADS) as i:
                enter(i, STEPS1)
                link(nc.vector.tensor_copy(slope[:, :], slopes[:, bass.ds(4 * i, 4)]))
                link(nc.vector.tensor_copy(taps[:, :], cols[:, bass.ds(3 * i + S_CONV, 3)]))
                for w in range(NBLK1):
                    split_1(i, 2 * w)
                    if 3 <= w < 7:
                        norm_a(i, w - 3)
                    if w == 4:
                        silu(i, 0, AZ)
                    if 11 <= w < 15:
                        norm_b(i, w - 11)
                    if w == 14:
                        silu(i, 1, BZ)
                    if w == 9:
                        dve.wait_ge(sd_ready, i + 1)
                        link(nc.vector.reciprocal(inv_a[:, :], inv_a[:, :]))
                        link(stt(o_a[:, :], o_a[:, :], gsub[:, :], inv_a[:, :], ALU.mult, ALU.mult))
                        dve.wait_ge(y_stored[0], 16 * i + 16)
                        stt(y_a[:, :], o_a[:, :], 0.5, blk[AZ][:, :], ALU.mult, ALU.mult).then_inc(y_ready, 1)
                    scale_block(i, w)
                    split_1(i, 2 * w + 1)
                    if 2 <= w < 6:
                        bias_a(i, w - 2)
                    if 10 <= w < 14:
                        bias_b(i, w - 10)
                    if w == 7:
                        dve.wait_ge(o_ready, 2 * i + 1)
                        nc.vector.tensor_copy(o_a[:, :], o_ps[:, :]).then_inc(o_free, 1)
                    if w == 8:
                        dve.wait_ge(s_ready, 9 * i + 5)
                        ts(sq_a[:, :], sc_ps[0][:, :], 1.0 / P, EPS, ALU.mult, ALU.add).then_inc(s_free, 1)
                    if w == 15:
                        dve.wait_ge(o_ready, 2 * i + 2)
                        dve.wait_ge(y_stored[1], 16 * i + 16)
                        stt(y_b[:, :].rearrange("p (b c) -> p b c", c=4), o_ps[:, :].rearrange("p (c b) -> p b c", c=4), 0.5,
                            blk[BZ][:, :].rearrange("p (b c) -> p b c", c=4), ALU.mult, ALU.mult).then_inc(o_free, 1)
                    if w == CX:
                        dve.wait_ge(evac_done, NBLK1 * i + (RING + CX + 1))
                        link(tt(u[:, 2:T + 2], blk[CC][:, :], blk[CX][:, :], ALU.mult))
                        link(ts(blk[CC][:, :], u[:, 2:T + 2], taps[:, 2:3], None, ALU.mult))
                        link(stt(blk[CC][:, :], u[:, 1:T + 1], taps[:, 1:2], blk[CC][:, :], ALU.mult, ALU.add))
                        link(stt(blk[CC][:, :], u[:, 0:T], taps[:, 0:1], blk[CC][:, :], ALU.mult, ALU.add))
                        link(tt(blk[CC][:, :], blk[CC][:, :], blk[CB][:, :], ALU.mult))
                    if w == CZ:
                        silu(i, 2, CZ)
                        dve.wait_ge(y_stored[2], 16 * i + 16)
                        stt(y_c[:, :], blk[CC][:, :], 0.5, blk[CZ][:, :], ALU.mult, ALU.mult).then_inc(y_ready, 1)
                leave(HEADS)

            def merge(j, t, used, gates):
                if t in (1, 3, 5):
                    b = t // 2
                    dve.wait_ge(pe_used, used)
                    tt(gate[b][:, :], pb[b][:, :], rstd[:, :], ALU.mult).then_inc(evac_done, 1)
                if t >= 6:
                    b = t - 6
                    dve.wait_ge(pe_used, used)
                    dve.wait_ge(gate_done, gates)
                    stt(gate[b][:, :], gate[b][:, :], 1.0, pb[b][:, :], ALU.add, ALU.mult).then_inc(evac_done, 1)
                    if b == 1:
                        dve.wait_ge(evac_done, NBLK2 * j + (NBLK1 * HEADS + RING + 5))
                        link(tt(gate[0][:, :], gate[0][:, :], gate[1][:, :], ALU.add))
                    if b == 2:
                        dve.wait_ge(evac_done, NBLK2 * j + (NBLK1 * HEADS + RING + 6))
                        dve.wait_ge(m_stored, 16 * j + 16)
                        tt(merged[:, :], gate[0][:, :], gate[2][:, :], ALU.add).then_inc(m_ready, 1)

            r = W1 + RING
            for t, tick in enumerate(first_merged_ring()):
                for n_item, (kind, n) in enumerate(tick):
                    if kind == "y":
                        split_lo_pair(r % RING, y_lo, y_hi, n, r + 1)
                    else:
                        split_lo(r % RING, n % RING, r + 1)
                    r += 1
                merge(0, t, W1 + RING + t + 1, 3)
            with dve.Fori(1, KT) as j:
                enter(j - 1, 1)
                for t in range(NHU2):
                    split_lo(t % RING, t % RING, NHU2 * j + (W1 + N_Y + RING + t + 1))
                    merge(j, t, NHU2 * j + (W1 + RING + t + 1), 3 * j + 3)
                leave(KT - 1)
            r = W1 + W2 + RING + N_Y
            for item in range(N_M):
                split_lo_pair((r + item) % RING, act_lo, act_hi, item, r + item + 1)
            r += N_M
            n = W1 + W2 + RING

            def add_residual(used, bank, blk_i):
                dve.wait_ge(pe_used, used)
                x_i = res[:, blk_i, :] if isinstance(blk_i, int) else res[:, bass.ds(blk_i, 1), :].rearrange("p o q -> p (o q)")
                stt(x_i, pb[bank][:, :], 0.5, x_i, ALU.mult, ALU.add).then_inc(evac_done, 1)

            for t in range(2):
                split_lo((r + t) % RING, (n + t) % RING, r + t + 1)
            dve.wait_ge(res_in, 16)
            add_residual(n + 2, 0, 0)

            def out_round(m, splits):
                for s in range(3):
                    for half in range(2):
                        t = 2 * s + half
                        if t < splits:
                            split_lo((r + 2 + t) % RING, (n + 2 + t) % RING, 6 * m + (r + 2 + t + 1))
                    add_residual(6 * m + (n + 2 + 2 * s + 2), (1 + s) % RING, 3 * m + (1 + s))

            with dve.Fori(0, 4) as m:
                out_round(m, 6)
            out_round(4, 3)
            dve.wait_ge(std_done, 2)
            link(nc.vector.reciprocal(frstd[:, :], frstd[:, :]))
            for k in range(KT):
                if k >= 4:
                    dve.wait_ge(out_stored[k % 4], 16 * (k // 4))
                stt(fin[k % 4][:, :], res[:, k, :], cols[:, S_FG + k:S_FG + k + 1], frstd[:, :], ALU.mult, ALU.mult).then_inc(fin_ready, 1)


def kernel(**inputs):
    import numpy as np
    import concourse.bacc as bacc
    from concourse.bass_utils import run_bass_kernel_spmd

    def get(name):
        return np.ascontiguousarray(inputs[name])

    const = np.zeros((P, C_END), np.float32)
    p = np.arange(P)[:, None]
    dist = p + (T - P) - np.arange(T)[None, :]
    const[:, C_MA:C_MA + T] = np.where(dist >= 0, dist, FAR)
    dist = 4 * p + 3 - np.arange(515)[None, :]
    const[:, C_M0:C_M0 + 515] = np.where((dist >= 0) & (dist <= 128), dist, FAR)
    dist = 4 * (p - np.arange(P)[None, :])
    const[:, C_M12:C_M12 + P] = np.where(dist >= 0, dist, FAR)
    const[:, C_M12 + P:C_M12 + 2 * P] = np.where((dist >= 0) & (dist % 16 == 0), dist, FAR)
    const[:, C_ID:C_ID + P] = np.eye(P)
    const[:, C_ONE:C_ONE + P] = 1.0
    slopes = 2.0 ** (-8.0 * np.arange(1, 4 * HEADS + 1) / (4 * HEADS))
    for h in range(HEADS):
        const[:, C_SL + 4 * h] = -slopes[h] / SCALE_A
        for g in range(3):
            const[:, C_SL + 4 * h + 1 + g] = -slopes[HEADS + g * HEADS + h] / SCALE_B

    def units(w, half):
        return w[half * 8 * P:(half + 1) * 8 * P].reshape(8, P, -1, P).transpose(2, 1, 0, 3).reshape(-1, P, HU)

    w_in = get("w_in")[0]
    wi = [units(w_in, half) for half in range(2)]
    wb = [units(get(f"w_branch_{x}")[0], 0) for x in "abc"]
    wo = [units(get("w_out")[0], half) for half in range(2)]
    nb = HEADS
    order = [0, nb, 2 * nb, 3 * nb]
    b0 = 4 * nb
    order += [b0, b0 + nb, b0 + 3 * nb, b0 + 4 * nb, b0 + 6 * nb, b0 + 7 * nb]
    order += [b0 + 2 * nb, b0 + 5 * nb, b0 + 8 * nb, b0 + 9 * nb]
    c0 = b0 + 10 * nb
    order += [c0, c0 + nb, c0 + 2 * nb, c0 + 3 * nb]
    g0 = c0 + 4 * nb
    wst = np.empty((W1 + W2 + W3, P, HU), np.float32)
    n = 0
    for h in range(HEADS):
        for b in order:
            for half in range(2):
                wst[n] = wi[half][b + h]
                n += 1
    for j in range(KT):
        for b in range(3):
            for half in range(2):
                wst[n] = wi[half][g0 + b * KT + j]
                n += 1
        for b in range(3):
            wst[n] = wb[b][j]
            n += 1
    for j in range(NBLK3):
        for half in range(2):
            wst[n] = wo[half][j]
            n += 1

    x_t = np.ascontiguousarray(get("x")[0].T).reshape(KT, P, T)
    cols = np.concatenate([
        get("norm_g")[0].reshape(KT, P).T,
        get("gate_b")[0].reshape(3, KT, P).transpose(2, 1, 0).reshape(P, 48),
        get("subln_g")[0].reshape(P, 1),
        get("conv_w")[0].reshape(3, HEADS, P).transpose(2, 1, 0).reshape(P, 24),
        get("final_g").reshape(KT, P).T], axis=1)
    lam = np.stack([get(f"lambda_{x}")[0] for x in ("q1", "k1", "q2", "k2")]).reshape(1, 256)
    arrays = {"wst": wst, "x_t": x_t, "cols_d": np.ascontiguousarray(cols), "lam_d": lam, "const_d": const}

    nc = bacc.Bacc("TRN2", target_bir_lowering=False, num_devices=1)
    args = [nc.dram_tensor(k, a.shape, mybir.dt.from_np(a.dtype), kind="ExternalInput").ap() for k, a in arrays.items()]
    args.append(nc.dram_tensor("out_0", (KT, P, T), mybir.dt.float32, kind="ExternalOutput").ap())
    program(nc, *args)
    r = run_bass_kernel_spmd(nc, [arrays], core_ids=[0])
    return r.results[0]["out_0"].reshape(D, T).T.reshape(1, T, D)
```

```python
import math
from contextlib import ExitStack

import concourse.bass as bass
from concourse import mybir

P = 128
D = 2048
T = 512
KT = D // P
HEADS = 8
HU = 8 * P
RING = 3
NBLK1, NBLK2, NBLK3 = 18, 6, 16
NHU1, NHU2 = 36, 9
W1 = HEADS * NHU1
W2 = KT * NHU2
W3 = 2 * NBLK3
LAM_INIT = 0.8 - 0.6 * math.exp(-0.3 * 0)
EPS = 1e-6
FAR = 1e30
SCALE_A = 64 ** -0.5
SCALE_B = 128 ** -0.5
C_MA, C_M0, C_M12, C_ID, C_ONE, C_SL = 0, 512, 512 + 515, 1283, 1283 + 128, 1283 + 256
C_END = C_SL + 4 * HEADS
S_G, S_GB, S_SUB, S_CONV, S_FG = 0, 16, 64, 65, 89
S_END = 105
Y_ITEMS = [1, 2, 2, 2, 2, 2, 1, 0, 0]
M_ITEMS = [0, 0, 0, 0, 0, 2, 2, 2, 2]
N_Y, N_M = 12, 8
AQ, AK, AV, AZ, Q0, K0, Q1, K1, Q2, K2, V0, V1, V2, BZ, CB, CC, CX, CZ = range(NBLK1)


def first_merged_ring():
    ticks, y = [], 0
    for t in range(NHU2):
        items = [("y", y + m) for m in range(Y_ITEMS[t])]
        y += Y_ITEMS[t]
        ticks.append(items + [("w", W1 + RING + t)])
    return ticks


def last_merged_ring():
    ticks, m = [], 0
    for t in range(NHU2):
        ticks.append([("w", W1 + (KT - 1) * NHU2 + RING + t)] + [("m", m + x) for x in range(M_ITEMS[t])])
        m += M_ITEMS[t]
    return ticks


R_FIRST = W1 + RING
R_LAST = W1 + N_Y + (KT - 1) * NHU2 + RING
PLACE = {x: R_FIRST + n for n, x in enumerate(x for tick in first_merged_ring() for x in tick)}
PLACE |= {x: R_LAST + n for n, x in enumerate(x for tick in last_merged_ring() for x in tick)}
R_OUT = R_LAST + NHU2 + N_M
SPLIT = [AQ, AK, Q0, K0, Q1, K1, Q2, K2]
STAGED = SPLIT + [AV, V0, V1, V2]
SPLIT_AT = (0, 6, 11)
BY_POOL = [3, 7, 11, 15]
BY_VECTOR = [k for k in range(KT) if k not in BY_POOL]


def program(nc, wst, x_t, cols_d, lam_d, const_d, out_d):
    f32, f32r = mybir.dt.float32, mybir.dt.float32r
    ALU, ACT, AX = mybir.AluOpType, mybir.ActivationFunctionType, mybir.AxisListType
    y_dram = nc.dram_tensor("y_dram", (3 * HEADS, P, T), f32, kind="Internal").ap()
    m_dram = nc.dram_tensor("m_dram", (KT, P, T), f32, kind="Internal").ap()

    with ExitStack() as ctx:
        def sb_in(c):
            return lambda name, shape, dt=f32: c.enter_context(nc.sbuf_tensor(name, shape, dt))

        def sem(name):
            return ctx.enter_context(nc.semaphore(name))

        sb = sb_in(ctx)
        act_hi, act_lo = sb("act_hi", [P, KT, T], f32r), sb("act_lo", [P, KT, T], f32r)
        raw = [sb(f"raw{i}", [P, HU]) for i in range(RING)]
        w_hi = [sb(f"w_hi{i}", [P, HU], f32r) for i in range(RING)]
        w_lo = [sb(f"w_lo{i}", [P, HU], f32r) for i in range(RING)]
        rstd = sb("rstd", [P, T])
        cols = sb("cols", [P, S_END])
        eps = sb("eps", [P, 1])
        lam_col = sb("lam_col", [P, 1])
        gsub = sb("gsub", [P, 1])
        ones = sb("ones", [P, P])
        ident = sb("ident", [P, P])

        with ExitStack() as c1:
            s1 = sb_in(c1)
            masks = s1("masks", [P, C_ID])
            slopes = s1("slopes", [P, 4 * HEADS])
            slope = s1("slope", [P, 4])
            taps = s1("taps", [P, 3])
            lam_in = s1("lam_in", [1, 4 * 64])
            lam_w = s1("lam_w", [1, 2 * 64])
            lam_s = s1("lam_s", [1, 8])
            nmax, sums, rsum = s1("nmax", [P, 2]), s1("sums", [P, 2]), s1("rsum", [P, 2])
            small_words = C_ID + 4 * HEADS + 7 + 6 * 64 + 8 + 6 + 64
            stage = [s1(f"stage{n}", [P, T]) for n in range(2)]
            z = s1("z", [P, T])
            cb, cc, cx = s1("cb", [P, T]), s1("cc", [P, T]), s1("cx", [P, T])
            blk = {b: stage[b % 2] for b in STAGED} | {AZ: z, BZ: z, CZ: z, CB: cb, CC: cc, CX: cx}
            qk_hi = {b: s1(f"qk_hi{b}", [P, T], f32r) for b in SPLIT[2:]}
            qk_lo = {b: s1(f"qk_lo{b}", [P, T], f32r) for b in SPLIT[2:]}
            for tiles in (qk_hi, qk_lo):
                tiles[AQ], tiles[AK] = tiles[Q1], tiles[K1]
            v_hi = [s1(f"v_hi{g}", [P, 4, P], f32r) for g in range(3)]
            v_lo = [s1(f"v_lo{g}", [P, 4, P], f32r) for g in range(3)]
            pt_hi, pt_lo = s1("pt_hi", [P, 24 * P], f32r), s1("pt_lo", [P, 24 * P], f32r)
            th, tmp_a, o_a = s1("th", [P, T]), s1("tmp_a", [P, T]), s1("o_a", [P, T])
            sq_a, inv_a = th, tmp_a
            sc, pr = s1("sc", [P, 2 * T]), s1("pr", [P, 6 * P])
            y_a, y_b = s1("y_a", [P, T]), s1("y_b", [P, T])
            y_c = y_b
            u = s1("u", [P, T + 2])
            sc_a = sc[:, :].rearrange("p (m q) -> p m q", m=2)
            pt_a = [t[:, 0:4 * T].rearrange("p (n q) -> p n q", n=4) for t in (pt_hi, pt_lo)]
            pt_b = [t[:, :].rearrange("p (n c b) -> p n c b", n=6, c=4) for t in (pt_hi, pt_lo)]
        with ExitStack() as c0:
            s0 = sb_in(c0)
            s0("below", [P, small_words])
            x_raw = s0("x_raw", [P, KT, T])
            xg = [s0(f"xg{i}", [P, T]) for i in range(2)]
            xsq = [s0(f"xsq{i}", [P, T]) for i in range(3)]
            xacc = s0("xacc", [P, T])
        with ExitStack() as c2:
            s2 = sb_in(c2)
            gate = [s2(f"gate{b}", [P, T]) for b in range(3)]
            merged = s2("merged", [P, T])
            y_hi, y_lo = s2("y_hi", [P, 3 * HEADS, T], f32r), s2("y_lo", [P, 3 * HEADS, T], f32r)
        with ExitStack() as c3:
            s3 = sb_in(c3)
            s3("kept", [P, 4 * T])
            res = s3("res", [P, KT, T])
            rsq = [s3(f"rsq{i}", [P, T]) for i in range(RING)]
            racc = s3("racc", [P, T])
            frstd = s3("frstd", [P, T])
            fcol = s3("fcol", [P, 4])

        pb = [ctx.enter_context(nc.psum_tensor(f"proj{i}", [P, T], f32)) for i in range(RING)]
        sc_ps = [ctx.enter_context(nc.psum_tensor(f"sc_ps{i}", [P, T], f32)) for i in range(2)]
        tr_ps = [ctx.enter_context(nc.psum_tensor(f"tr_ps{i}", [P, T], f32)) for i in range(2)]
        o_ps = ctx.enter_context(nc.psum_tensor("o_ps", [P, T], f32))

        cols_in, const_in = sem("cols_in"), sem("const_in")
        x_in = [sem(f"x_in{i}") for i in range(8)]
        res_in = sem("res_in")
        raw_in = [sem(f"raw_in{i}") for i in range(RING)]
        y_stored = [sem(f"y_stored{b}") for b in range(3)]
        m_stored = sem("m_stored")
        out_stored = sem("out_stored")
        hi_done, lo_done, pe_used = sem("hi_done"), sem("lo_done"), sem("pe_used")
        evac_done = sem("evac_done")
        xg_done, xh_done, xl_done = sem("xg_done"), sem("xh_done"), sem("xl_done")
        xsq_done, xacc_add, ss_done, std_done = sem("xsq_done"), sem("xacc_add"), sem("ss_done"), sem("std_done")
        qh_done, ql_done, t_hi = sem("qh_done"), sem("ql_done"), sem("t_hi")
        m15_hi, m15_lo = sem("m15_hi"), sem("m15_lo")
        lam_sum, lam_exp, lam_set, lam_bc = sem("lam_sum"), sem("lam_exp"), sem("lam_set"), sem("lam_bc")
        s_ready, s_free = sem("s_ready"), sem("s_free")
        t_ready, t_free = sem("t_ready"), sem("t_free")
        o_ready, o_free = sem("o_ready"), sem("o_free")
        biased, exp_done, p_ready = sem("biased"), sem("exp_done"), sem("p_ready")
        th_ready, sq_ready, sd_ready, y_ready = sem("th_ready"), sem("sq_ready"), sem("sd_ready"), sem("y_ready")
        gate_done, m_ready = sem("gate_done"), sem("m_ready")
        rsq_done, racc_done, rg_done = sem("rsq_done"), sem("racc_done"), sem("rg_done")
        fcol_done, frstd_ps, frstd_done, fin_ready = sem("fcol_done"), sem("frstd_ps"), sem("frstd_done"), sem("fin_ready")
        fin_pool = sem("fin_pool")
        dve_step = sem("dve_step")

        block = ctx.enter_context(nc.Block())

        def natural(ap):
            return ap

        def by_class(ap):
            return ap.rearrange("p (b c) -> p c b", c=4)

        def as_class(ap):
            return ap.rearrange("p (c b) -> p c b", c=4)

        @block.sync
        def _(sp):
            def load_w(slot, n):
                src = wst[n, :, :] if isinstance(n, int) else wst[bass.ds(n, 1), :, :].rearrange("o p f -> p (o f)")
                sp.dma_start(raw[slot][:, :], src).then_inc(raw_in[slot], 16)

            def load_pair(slot, dram, item):
                sp.dma_start(raw[slot][:, :].rearrange("p (t q) -> p t q", t=2),
                             dram[2 * item:2 * item + 2, :, :].rearrange("t p q -> p t q")).then_inc(raw_in[slot], 16)

            for r in range(RING):
                load_w(r, r)
            with sp.Fori(1, W1 // RING + 1) as i:
                for s in range(RING):
                    sp.wait_ge(lo_done, RING * i + s - RING + 1)
                    load_w(s, RING * i + s)
            for b in range(3):
                sp.wait_ge(y_stored[b], 16 * (HEADS + 1))
            r = W1 + RING
            for kind, n in [x for tick in first_merged_ring() for x in tick]:
                sp.wait_ge(lo_done, r - RING + 1)
                if kind == "y":
                    load_pair(r % RING, y_dram, n)
                else:
                    load_w(r % RING, n)
                r += 1
            n0 = W1 + NHU2 + RING
            with sp.Fori(0, (KT - 2) * NHU2 // RING) as i:
                for s in range(RING):
                    sp.wait_ge(lo_done, RING * i + (r + s - RING + 1))
                    load_w((r + s) % RING, RING * i + (n0 + s))
            r += (KT - 2) * NHU2
            for kind, n in [x for tick in last_merged_ring() for x in tick]:
                sp.wait_ge(lo_done, r - RING + 1)
                if kind == "m" and n < N_M - 1:
                    sp.wait_ge(m_stored, 16 * (2 * n + 3))
                    load_pair(r % RING, m_dram, n)
                elif kind == "m":
                    sp.wait_ge(m_stored, 16 * KT)
                    sp.dma_start(raw[r % RING][:, 0:T], m_dram[KT - 2, :, :]).then_inc(raw_in[r % RING], 16)
                else:
                    load_w(r % RING, n)
                r += 1
            n0 = W1 + W2 + RING
            left = W3 - RING
            with sp.Fori(0, left // RING) as i:
                for s in range(RING):
                    sp.wait_ge(lo_done, RING * i + (r + s - RING + 1))
                    load_w((r + s) % RING, RING * i + (n0 + s))
            for s in range(left - left % RING, left):
                sp.wait_ge(lo_done, r + s - RING + 1)
                load_w((r + s) % RING, n0 + s)

            for n, k in enumerate(BY_POOL):
                sp.wait_ge(fin_pool, n + 1)
                sp.dma_start(out_d[k, :, :], res[:, k, :]).then_inc(out_stored, 16)
            sp.wait_ge(out_stored, 16 * KT)

        @block.gpsimd
        def _(pool):
            for k in range(1, KT):
                pool.wait_ge(xsq_done, k + 1)
                if k > 1:
                    pool.wait_ge(xacc_add, k - 1)
                nc.gpsimd.tensor_tensor(xacc[:, :], (xsq[0] if k == 1 else xacc)[:, :], xsq[k % 3][:, :],
                                        ALU.add).then_inc(xacc_add, 1)
            pool.wait_ge(rsq_done, 1)
            nc.gpsimd.tensor_copy(racc[:, :], rsq[0][:, :]).then_inc(racc_done, 1)

            def add_squares(m, s):
                pool.wait_ge(rsq_done, 3 * m + (2 + s))
                pool.wait_ge(racc_done, 3 * m + (1 + s))
                nc.gpsimd.tensor_tensor(racc[:, :], racc[:, :], rsq[(1 + s) % RING][:, :], ALU.add).then_inc(racc_done, 1)

            with pool.Fori(0, 4) as m:
                for s in range(3):
                    add_squares(m, s)
            for s in range(2):
                add_squares(4, s)
            pool.wait_ge(frstd_done, 1)
            for k in BY_POOL:
                nc.gpsimd.tensor_tensor(res[:, k, :], res[:, k, :], frstd[:, :], ALU.mult).then_inc(fin_pool, 1)

        @block.tensor
        def _(pe):
            pe.sem_inc(pe_used, RING)

            def three(out, w_h, w_l, a_h, a_l, first, last):
                nc.tensor.matmul(out, w_h, a_h, start=first, stop=False)
                nc.tensor.matmul(out, w_h, a_l, start=False, stop=False)
                return nc.tensor.matmul(out, w_l, a_h, start=False, stop=last)

            def multiply(bank, slot, m_hi, m_lo, k0, first, last, fresh=False):
                for k in range(8):
                    if fresh:
                        pe.wait_ge(xl_done, k0 + k + 1)
                    ws = slice(k * P, (k + 1) * P)
                    end = three(pb[bank][:, :], w_hi[slot][:, ws], w_lo[slot][:, ws], m_hi[:, k0 + k, :],
                                m_lo[:, k0 + k, :], first and k == 0, last and k == 7)
                end.then_inc(pe_used, 1)

            def scaled(i, b):
                pe.wait_ge(evac_done, NBLK1 * i + (RING + b + 1))

            def split_ready(i, b):
                pe.wait_ge(ql_done, 8 * i + (SPLIT.index(b) + 1))

            def scores_a(i, q):
                n = P * (q + 1)
                split_ready(i, AK)
                pe.wait_ge(s_free, 9 * i + (q + 1))
                for m in range(2):
                    rows, qs = slice(64 * m, 64 * m + 64), slice(P * q, P * q + P)
                    end = three(sc_ps[m][:, 0:n], qk_hi[AQ][rows, qs], qk_lo[AQ][rows, qs],
                                qk_hi[AK][rows, 0:n], qk_lo[AK][rows, 0:n], True, True)
                end.then_inc(s_ready, 1)

            def turn(i, idx, tiles):
                pe.wait_ge(t_free, 16 * i + (idx + 1))
                for n, tile in enumerate(tiles):
                    end = nc.tensor.transpose(tr_ps[idx % 2][:, n * P:(n + 1) * P], tile, ident[:, :])
                end.then_inc(t_ready, 1)

            def probs_a(i, q):
                pe.wait_ge(p_ready, 8 * i + (q + 1))
                turn(i, 1 + q, [pr[:, n * P:(n + 1) * P] for n in range(q + 1)])

            def values_a(i):
                pe.wait_ge(t_free, 16 * i + (2 + 5))
                pe.wait_ge(o_free, 2 * i + 1)
                for n in range(4):
                    end = three(o_ps[:, n * P:T], v_hi[0][:, n, :], v_lo[0][:, n, :], pt_a[0][:, n, n * P:T],
                                pt_a[1][:, n, n * P:T], n == 0, n == 3)
                end.then_inc(o_ready, 1)

            def squares_a(i):
                pe.wait_ge(sq_ready, i + 1)
                pe.wait_ge(s_free, 9 * i + 5)
                nc.tensor.matmul(sc_ps[0][:, :], ones[:, :], sq_a[:, :], start=True, stop=True).then_inc(s_ready, 1)

            def scores_b(i, c):
                split_ready(i, K2)
                pe.wait_ge(s_free, 9 * i + (6 + c))
                qs = slice(c * P, (c + 1) * P)
                for g, (q, k) in enumerate(((Q0, K0), (Q1, K1), (Q2, K2))):
                    out = sc_ps[0][:, :] if g == 0 else sc_ps[1][:, (g - 1) * P:g * P]
                    ks = slice(0, T) if g == 0 else qs
                    end = three(out, qk_hi[q][:, qs], qk_lo[q][:, qs], qk_hi[k][:, ks], qk_lo[k][:, ks], True, True)
                end.then_inc(s_ready, 1)

            first_turn = [5, 8, 11, 14]

            def probs_b(i, c):
                pe.wait_ge(p_ready, 8 * i + (5 + c))
                turn(i, first_turn[c], [pr[:, n * P:(n + 1) * P] for n in range(4)])
                turn(i, first_turn[c] + 1, [pr[:, n * P:(n + 1) * P] for n in range(4, 6)])

            def values_b(i):
                pe.wait_ge(t_free, 16 * i + (2 + 16))
                pe.wait_ge(o_free, 2 * i + 2)
                for g in (1, 2):
                    for c in range(4):
                        three(o_ps[:, c * P:(c + 1) * P], v_hi[g][:, c, :], v_lo[g][:, c, :], pt_b[0][:, 3 + g, c, :],
                              pt_b[1][:, 3 + g, c, :], g == 1 and c == 0, False)
                for n in range(4):
                    bs = slice(32 * n, min(32 * n + 64, P))
                    end = three(as_class(o_ps[:, :])[:, :, bs], v_hi[0][:, n, :], v_lo[0][:, n, :], pt_b[0][:, n, :, bs],
                                pt_b[1][:, n, :, bs], False, n == 3)
                end.then_inc(o_ready, 1)

            def quarter(tile):
                return [tile[:, n * P:(n + 1) * P] for n in range(4)]

            def head(i):
                fresh = isinstance(i, int)
                for w in range(NBLK1):
                    pe.wait_ge(evac_done, NBLK1 * i + (w + 1))
                    pe.wait_ge(lo_done, NHU1 * i + (2 * w + 1))
                    multiply(w % RING, 2 * w % RING, act_hi, act_lo, 0, True, False, fresh and w == 0)
                    if w == 12:
                        scaled(i, V0)
                        turn(i, 7, quarter(blk[V0]))
                    if w == 13:
                        scaled(i, V1)
                        turn(i, 10, quarter(blk[V1]))
                    if w == 14:
                        scaled(i, V2)
                        turn(i, 13, quarter(blk[V2]))
                    pe.wait_ge(lo_done, NHU1 * i + (2 * w + 2))
                    multiply(w % RING, (2 * w + 1) % RING, act_hi, act_lo, 8, False, True, fresh and w == 0)
                    if fresh and w == 0:
                        pe.wait_ge(cols_in, 16 * 3)
                        pe.wait_ge(xacc_add, KT - 1)
                        nc.tensor.matmul(o_ps[:, :], ones[:, :], xacc[:, :], start=True, stop=True).then_inc(ss_done, 1)
                        pe.wait_ge(lam_set, 1)
                        pe.wait_ge(const_in, 16 * 3)
                        nc.tensor.matmul(tr_ps[0][:, 0:1], ones[0:1, :], lam_s[0:1, 4:5], start=True,
                                         stop=True).then_inc(lam_bc, 1)
                    if 2 <= w < 6:
                        scores_a(i, w - 2)
                    if w == 3:
                        scaled(i, AV)
                        turn(i, 0, quarter(blk[AV]))
                    if 3 <= w < 7:
                        probs_a(i, w - 3)
                    if w == 7:
                        values_a(i)
                    if w == 8:
                        squares_a(i)
                    if 10 <= w < 14:
                        scores_b(i, w - 10)
                    if 11 <= w < 15:
                        probs_b(i, w - 11)
                    if w == 15:
                        values_b(i)

            head(0)
            with pe.Fori(1, HEADS) as i:
                head(i)

            def merge_block(evac, ready, y_needed=(0, 0, 0)):
                for b in range(3):
                    pe.wait_ge(evac_done, evac + (b + 1))
                    for half in range(2):
                        pe.wait_ge(lo_done, ready[2 * b + half])
                        multiply(b, (2 * b + half) % RING, act_hi, act_lo, 8 * half, half == 0, half == 1)
                for b in range(3):
                    pe.wait_ge(evac_done, evac + (b + 4))
                    pe.wait_ge(lo_done, ready[6 + b])
                    if y_needed[b]:
                        pe.wait_ge(lo_done, y_needed[b])
                    multiply(b, (6 + b) % RING, y_hi, y_lo, 8 * b, True, True)

            evac0 = NBLK1 * HEADS
            merge_block(evac0, [W1 + t + 1 if t < RING else PLACE["w", W1 + t] + 1 for t in range(NHU2)],
                        [PLACE["y", 4 * b + 3] + 1 for b in range(3)])
            with pe.Fori(1, KT - 1) as j:
                merge_block(NBLK2 * j + evac0, [NHU2 * j + (W1 + N_Y + t + 1) for t in range(NHU2)])
            n_last = W1 + (KT - 1) * NHU2
            merge_block(NBLK2 * (KT - 1) + evac0,
                        [n_last + N_Y + t + 1 if t < RING else PLACE["w", n_last + t] + 1 for t in range(NHU2)])

            evac0 += NBLK2 * KT
            n0 = W1 + W2

            def out_block(bank, slot, evac, ready):
                pe.wait_ge(evac_done, evac + 1)
                for half in range(2):
                    for sem_, value in ready[half]:
                        pe.wait_ge(sem_, value)
                    multiply(bank, (slot + half) % RING, act_hi, act_lo, 8 * half, half == 0, half == 1)

            out_block(0, 0, evac0, [[(lo_done, PLACE["w", n0] + 1), (lo_done, PLACE["m", 3] + 1)],
                                    [(lo_done, PLACE["w", n0 + 1] + 1), (lo_done, PLACE["m", 7] + 1), (m15_lo, 1)]])

            def out_round(m):
                for s in range(3):
                    at = [R_OUT + 2 * s + half for half in range(2)]
                    ready = [[(lo_done, 6 * m + x)] for x in at]
                    out_block((1 + s) % RING, (2 + 2 * s) % RING, 3 * m + (evac0 + 1 + s), ready)

            with pe.Fori(0, 5) as m:
                out_round(m)
            pe.wait_ge(racc_done, NBLK3 - 1)
            for n in range(4):
                nc.tensor.matmul(tr_ps[0][:, n:n + 1], racc[:, n * P:(n + 1) * P], ones[:, 0:1], start=n == 0, stop=False,
                                 skip_group_check=True)
            pe.wait_ge(rsq_done, NBLK3)
            for n in range(4):
                end = nc.tensor.matmul(tr_ps[0][:, n:n + 1], rsq[(NBLK3 - 1) % RING][:, n * P:(n + 1) * P], ones[:, 0:1],
                                       start=False, stop=True, skip_group_check=True)
            end.then_inc(ss_done, 1)
            pe.wait_ge(fcol_done, 1)
            for n in range(4):
                end = nc.tensor.matmul(o_ps[:, n * P:(n + 1) * P], fcol[:, n:n + 1].to_broadcast([P, P]), ident[:, :],
                                       start=True, stop=True)
            end.then_inc(frstd_ps, 1)

        @block.scalar
        def _(act):
            act.dma_start(cols[:, :], cols_d).then_inc(cols_in, 16)
            act.dma_start(lam_in[:, :], lam_d).then_inc(cols_in, 16)
            act.dma_start(ones[:, :], const_d[:, C_ONE:C_ONE + P]).then_inc(cols_in, 16)
            for g in range(8):
                act.dma_start(x_raw[:, 2 * g:2 * g + 2, :], x_t[2 * g:2 * g + 2, :, :].rearrange("k p t -> p k t")).then_inc(x_in[g], 16)
            act.dma_start(masks[:, :], const_d[:, 0:C_ID]).then_inc(const_in, 16)
            act.dma_start(ident[:, :], const_d[:, C_ID:C_ID + P]).then_inc(const_in, 16)
            act.dma_start(slopes[:, :], const_d[:, C_SL:C_END]).then_inc(const_in, 16)
            for b in range(3):
                act.sem_inc(y_stored[b], 16)
            act.sem_inc(m_stored, 16)

            def split_hi(slot_raw, slot_w, used, loads):
                act.wait_ge(raw_in[slot_raw], 16 * loads)
                act.wait_ge(pe_used, used)
                nc.scalar.activation(w_hi[slot_w][:, :], raw[slot_raw][:, :], ACT.Copy).then_inc(hi_done, 1)

            def split_hi_pair(slot_raw, dst, item, loads):
                act.wait_ge(raw_in[slot_raw], 16 * loads)
                nc.scalar.activation(dst[:, 2 * item:2 * item + 2, :].rearrange("p t q -> p (t q)"),
                                     raw[slot_raw][:, :], ACT.Copy).then_inc(hi_done, 1)

            for k in range(KT):
                act.wait_ge(x_in[k // 2], 16)
                if k >= 3:
                    act.wait_ge(xacc_add, max(k - 3, 1))
                nc.scalar.activation(xsq[k % 3][:, :], x_raw[:, k, :], ACT.Square).then_inc(xsq_done, 1)
                act.wait_ge(xg_done, k + 1)
                nc.scalar.activation(act_hi[:, k, :], xg[k % 2][:, :], ACT.Copy).then_inc(xh_done, 1)
                if k in SPLIT_AT:
                    n = SPLIT_AT.index(k)
                    split_hi(n, n, n + 1, 1)
                if k == 2:
                    act.wait_ge(lam_sum, 1)
                    nc.scalar.activation(lam_s[0:1, 2:4], lam_s[0:1, 0:2], ACT.Exp).then_inc(lam_exp, 1)
            act.wait_ge(ss_done, 1)
            nc.scalar.activation(rstd[:, :], o_ps[:, :], ACT.Sqrt, scale=1.0 / D, bias=eps[:, :]).then_inc(std_done, 1)

            def split_1(i, t):
                split_hi(t % RING, t % RING, NHU1 * i + (t + RING + 1), (NHU1 // RING) * i + (t // RING + 2))

            def exps(i, idx, tile, spans, scale):
                act.wait_ge(biased, 8 * i + (idx + 1))
                for m, (lo, hi) in enumerate(spans):
                    end = nc.scalar.activation(tile[:, lo:hi], tile[:, lo:hi], ACT.Exp, scale=scale,
                                               bias=nmax[:, m:m + 1], accum_out=sums[:, m:m + 1])
                end.then_inc(exp_done, 1)

            def turned(i, idx, dst, n):
                act.wait_ge(t_ready, 16 * i + (idx + 1))
                nc.scalar.activation(dst, tr_ps[idx % 2][:, 0:n * P].rearrange("p (n q) -> p n q", n=n),
                                     ACT.Copy).then_inc(t_hi, 1)

            def split_block(i, w):
                act.wait_ge(evac_done, NBLK1 * i + (RING + w + 1))
                nc.scalar.activation(qk_hi[w][:, :], blk[w][:, :], ACT.Copy).then_inc(qh_done, 1)

            def tanh_half(i, w):
                act.wait_ge(evac_done, NBLK1 * i + (RING + w + 1))
                nc.scalar.activation(th[:, :], blk[w][:, :], ACT.Tanh, scale=0.5).then_inc(th_ready, 1)

            def store_y(i, b, tile):
                act.dma_start(y_dram[bass.ds(i + HEADS * b, 1), :, :].rearrange("o p q -> p (o q)"), tile[:, :]).then_inc(y_stored[b], 16)

            first_turn = [5, 8, 11, 14]
            with act.Fori(0, HEADS) as i:
                for w in range(NBLK1):
                    split_1(i, 2 * w)
                    if 12 <= w < 15:
                        turned(i, first_turn[w - 12] + 2, v_hi[w - 12][:, :, :], 4)
                    if w in SPLIT:
                        split_block(i, w)
                    split_1(i, 2 * w + 1)
                    if w == 3:
                        turned(i, 0, v_hi[0][:, :, :], 4)
                    if 3 <= w < 7:
                        q = w - 3
                        turned(i, 1 + q, pt_a[0][:, 0:q + 1, q * P:(q + 1) * P], q + 1)
                    if 11 <= w < 15:
                        c = w - 11
                        turned(i, first_turn[c], pt_b[0][:, 0:4, c, :], 4)
                        turned(i, first_turn[c] + 1, pt_b[0][:, 4:6, c, :], 2)
                    if 2 <= w < 6:
                        q = w - 2
                        exps(i, q, sc, [(m * T, m * T + P * (q + 1)) for m in range(2)], SCALE_A)
                    if 10 <= w < 14:
                        exps(i, 4 + w - 10, sc, [(0, 6 * P)], SCALE_B)
                    if w in (AZ, BZ, CZ):
                        tanh_half(i, w)
                    if w == 7:
                        act.wait_ge(o_free, 2 * i + 2)
                        nc.scalar.activation(sq_a[:, :], o_a[:, :], ACT.Square).then_inc(sq_ready, 1)
                    if w == 8:
                        act.wait_ge(s_free, 9 * i + 6)
                        nc.scalar.activation(inv_a[:, :], sq_a[:, :], ACT.Sqrt).then_inc(sd_ready, 1)
                    if w == 9:
                        act.wait_ge(y_ready, 2 * i + 1)
                        store_y(i, 0, y_a)
                    if w == 15:
                        act.wait_ge(o_free, 2 * i + 3)
                        store_y(i, 1, y_b)
                    if w == CZ:
                        act.wait_ge(y_ready, 2 * i + 2)
                        store_y(i, 2, y_c)

            def tanh_gate(done, b, col):
                act.wait_ge(evac_done, done)
                nc.scalar.activation(gate[b][:, :], gate[b][:, :], ACT.Tanh, scale=0.5, bias=col).then_inc(gate_done, 1)

            evac0 = NBLK1 * HEADS + RING

            r = W1 + RING
            for t, tick in enumerate(first_merged_ring()):
                for kind, n in tick:
                    if kind == "y":
                        split_hi_pair(r % RING, y_hi, n, r // RING + 1)
                    else:
                        split_hi(r % RING, n % RING, n + 1, r // RING + 1)
                    r += 1
                if t in (1, 3, 5):
                    b = t // 2
                    tanh_gate(evac0 + b + 1, b, cols[:, S_GB + b:S_GB + b + 1])
            act.wait_ge(m_ready, 1)
            act.dma_start(m_dram[0, :, :], merged[:, :]).then_inc(m_stored, 16)
            with act.Fori(1, KT - 1) as j:
                for t in range(NHU2):
                    split_hi(t % RING, t % RING, NHU2 * j + (W1 + RING + t + 1),
                             (NHU2 // RING) * j + ((W1 + N_Y + RING + t) // RING + 1))
                    if t in (1, 3, 5):
                        b = t // 2
                        tanh_gate(NBLK2 * j + (evac0 + b + 1), b, cols[:, bass.ds(3 * j + (S_GB + b), 1)])
                act.wait_ge(m_ready, j + 1)
                act.dma_start(m_dram[bass.ds(j, 1), :, :].rearrange("o p q -> p (o q)"), merged[:, :]).then_inc(m_stored, 16)
            r = R_LAST
            for t, tick in enumerate(last_merged_ring()):
                for kind, n in tick:
                    if kind == "w":
                        split_hi(r % RING, n % RING, n + 1, r // RING + 1)
                    elif n < N_M - 1:
                        split_hi_pair(r % RING, act_hi, n, r // RING + 1)
                    else:
                        act.wait_ge(raw_in[r % RING], 16 * (r // RING + 1))
                        nc.scalar.activation(act_hi[:, KT - 2, :], raw[r % RING][:, 0:T], ACT.Copy).then_inc(hi_done, 1)
                    r += 1
                if t in (1, 3, 5):
                    b = t // 2
                    tanh_gate(NBLK2 * (KT - 1) + evac0 + b + 1, b, cols[:, S_GB + 45 + b:S_GB + 46 + b])
            act.wait_ge(m_stored, 16 * KT)
            act.wait_ge(pe_used, W1 + W2 + RING)
            act.dma_start(res[:, :, :], x_t.rearrange("k p t -> p k t")).then_inc(res_in, 16)
            act.wait_ge(m_ready, KT)
            nc.scalar.activation(act_hi[:, KT - 1, :], merged[:, :], ACT.Copy).then_inc(m15_hi, 1)
            r, n = R_OUT, W1 + W2 + RING

            def split_3(m, t):
                a, b = r + 2 + t, n + 2 + t
                split_hi(a % RING, b % RING, 6 * m + (b + 1), 2 * m + (a // RING + 1))

            def square_out(evac, k, s, rounds):
                if isinstance(k, int):
                    x_k, g_k = res[:, k, :], cols[:, S_FG + k:S_FG + k + 1]
                else:
                    x_k = res[:, bass.ds(k, 1), :].rearrange("p o q -> p (o q)")
                    g_k = cols[:, bass.ds(k + S_FG, 1)]
                if rounds is not None:
                    act.wait_ge(racc_done, rounds)
                act.wait_ge(evac_done, evac)
                nc.scalar.activation(rsq[s][:, :], x_k, ACT.Square).then_inc(rsq_done, 1)
                act.wait_ge(rsq_done, k + 1)
                nc.scalar.activation(x_k, x_k, ACT.Copy, scale=g_k).then_inc(rg_done, 1)

            evac1 = NBLK1 * HEADS + NBLK2 * KT + RING
            for t in range(2):
                a, b = r + t, n + t
                split_hi(a % RING, b % RING, b + 1, a // RING + 1)
            square_out(evac1 + 1, 0, 0, None)

            def out_round(m, splits):
                for s in range(3):
                    for half in range(2):
                        if 2 * s + half < splits:
                            split_3(m, 2 * s + half)
                    k = 3 * m + (1 + s)
                    square_out(3 * m + (evac1 + 2 + s), k, (1 + s) % RING,
                               None if isinstance(m, int) and k < RING else 3 * m + (s - 1))

            out_round(0, 6)
            with act.Fori(1, 4) as m:
                out_round(m, 6)
            out_round(4, 3)
            act.wait_ge(ss_done, 2)
            nc.scalar.activation(fcol[:, :], tr_ps[0][:, 0:4], ACT.Sqrt, scale=1.0 / D, bias=eps[:, :]).then_inc(std_done, 1)
            act.wait_ge(frstd_ps, 1)
            nc.scalar.activation(frstd[:, :], o_ps[:, :], ACT.Copy).then_inc(frstd_done, 1)
            for n, k in enumerate(BY_VECTOR):
                act.wait_ge(fin_ready, n + 1)
                act.dma_start(out_d[k, :, :], res[:, k, :]).then_inc(out_stored, 16)

        @block.vector
        def _(dve):
            steps = {"base": 0, "n": 0, "i": 0, "per": 0}

            def link(ins):
                steps["n"] += 1
                ins.then_inc(dve_step, 1)
                done = steps["base"] + steps["n"]
                dve.wait_ge(dve_step, steps["per"] * steps["i"] + done if steps["per"] else done)

            def enter(i, per):
                steps.update(i=i, per=per, base=steps["base"] + steps["n"], n=0)

            def leave(count):
                assert steps["n"] == steps["per"], steps
                steps.update(base=steps["base"] + steps["per"] * count, n=0, i=0, per=0)

            tt, ts, stt = nc.vector.tensor_tensor, nc.vector.tensor_scalar, nc.vector.scalar_tensor_tensor
            dve.sem_inc(evac_done, RING)
            dve.sem_inc(s_free, 1)
            dve.sem_inc(o_free, 1)
            dve.sem_inc(t_free, 2)
            nc.vector.memset(eps[:, :], EPS)
            nc.vector.memset(u[:, 0:2], 0.0)
            def split_lo(slot_raw, slot_w, hi):
                dve.wait_ge(hi_done, hi)
                tt(w_lo[slot_w][:, :], raw[slot_raw][:, :], w_hi[slot_w][:, :].bitcast(f32), ALU.subtract).then_inc(lo_done, 1)

            def split_lo_pair(slot_raw, lo, hi_part, item, hi):
                dve.wait_ge(hi_done, hi)
                tt(lo[:, 2 * item:2 * item + 2, :].rearrange("p t q -> p (t q)"), raw[slot_raw][:, :],
                   hi_part[:, 2 * item:2 * item + 2, :].rearrange("p t q -> p (t q)").bitcast(f32), ALU.subtract).then_inc(lo_done, 1)

            def x_low(k):
                dve.wait_ge(xh_done, k + 1)
                tt(act_lo[:, k, :], xg[k % 2][:, :], act_hi[:, k, :].bitcast(f32), ALU.subtract).then_inc(xl_done, 1)

            dve.wait_ge(cols_in, 16 * 3)
            lam_v = lam_in[:, :].rearrange("o (a b d) -> o a b d", a=2, b=2)
            link(tt(lam_w[:, :].rearrange("o (a d) -> o a d", a=2), lam_v[:, :, 0, :], lam_v[:, :, 1, :], ALU.mult))
            nc.vector.reduce_sum(lam_s[:, 0:2], lam_w[:, :].rearrange("o (a d) -> o a d", a=2), AX.X).then_inc(lam_sum, 1)
            ts(gsub[:, :], cols[:, S_SUB:S_SUB + 1], 1.0 - LAM_INIT, None, ALU.mult)
            link(ts(cols[:, S_GB:S_GB + 48], cols[:, S_GB:S_GB + 48], 0.5, None, ALU.mult))
            for k in range(KT):
                dve.wait_ge(x_in[k // 2], 16)
                if k >= 2:
                    dve.wait_ge(xl_done, k - 1)
                ts(xg[k % 2][:, :], x_raw[:, k, :], cols[:, S_G + k:S_G + k + 1], None, ALU.mult).then_inc(xg_done, 1)
                if k >= 1:
                    if k - 1 in SPLIT_AT:
                        n = SPLIT_AT.index(k - 1)
                        split_lo(n, n, n + 1)
                    x_low(k - 1)
                if k == 8:
                    dve.wait_ge(lam_exp, 1)
                    link(tt(lam_s[:, 6:7], lam_s[:, 2:3], lam_s[:, 3:4], ALU.subtract))
                    ts(lam_s[:, 4:5], lam_s[:, 6:7], LAM_INIT, None, ALU.add).then_inc(lam_set, 1)
            x_low(KT - 1)
            dve.wait_ge(const_in, 16 * 3)
            dve.wait_ge(lam_bc, 1)
            nc.vector.tensor_copy(lam_col[:, :], tr_ps[0][:, 0:1])
            dve.wait_ge(std_done, 1)
            link(nc.vector.reciprocal(rstd[:, :], rstd[:, :]))

            def split_1(i, t):
                split_lo(t % RING, t % RING, NHU1 * i + (t + RING + 1))

            classed = {Q0, Q1, K1, Q2, K2, V1, V2}

            def scale_block(i, w):
                dve.wait_ge(pe_used, NHU1 * i + (2 * w + 2 + RING))
                if w in classed:
                    ins = tt(as_class(blk[w][:, :]), by_class(pb[w % RING][:, :]), by_class(rstd[:, :]), ALU.mult)
                else:
                    ins = tt(blk[w][:, :], pb[w % RING][:, :], rstd[:, :], ALU.mult)
                ins.then_inc(evac_done, 1)

            def bias_a(i, q):
                n = P * (q + 1)
                dve.wait_ge(s_ready, 9 * i + (q + 1))
                if q:
                    dve.wait_ge(p_ready, 8 * i + q)
                for m in range(2):
                    end = stt(sc_a[:, m, 0:n], masks[:, C_MA + T - n:C_MA + T], slope[:, 0:1], sc_ps[m][:, 0:n], ALU.mult, ALU.add)
                end.then_inc(s_free, 1)
                dve.wait_ge(s_free, 9 * i + (q + 2))
                link(nc.vector.reduce_max(rsum[:, :], sc_a[:, :, 0:n], AX.X))
                ts(nmax[:, :], rsum[:, :], -SCALE_A, None, ALU.mult).then_inc(biased, 1)

            def norm_a(i, q):
                n = P * (q + 1)
                dve.wait_ge(exp_done, 8 * i + (q + 1))
                link(nc.vector.reciprocal(rsum[:, :], sums[:, :]))
                link(tt(rsum[:, 1:2], rsum[:, 1:2], lam_col[:, :], ALU.mult))
                link(ts(tmp_a[:, 0:n], sc_a[:, 1, 0:n], rsum[:, 1:2], None, ALU.mult))
                stt(pr[:, 0:n], sc_a[:, 0, 0:n], rsum[:, 0:1], tmp_a[:, 0:n], ALU.mult, ALU.subtract).then_inc(p_ready, 1)

            def bias_b(i, c):
                dve.wait_ge(s_ready, 9 * i + (6 + c))
                if c:
                    dve.wait_ge(p_ready, 8 * i + (4 + c))
                m0 = C_M0 + 3 - c
                stt(sc[:, 0:T], masks[:, m0:m0 + T], slope[:, 1:2], sc_ps[0][:, :], ALU.mult, ALU.add)
                for g in (1, 2):
                    end = stt(sc[:, (3 + g) * P:(4 + g) * P], masks[:, C_M12 + (g - 1) * P:C_M12 + g * P],
                              slope[:, 1 + g:2 + g], sc_ps[1][:, (g - 1) * P:g * P], ALU.mult, ALU.add)
                end.then_inc(s_free, 1)
                dve.wait_ge(s_free, 9 * i + (7 + c))
                link(nc.vector.reduce_max(rsum[:, 0:1], sc[:, 0:6 * P], AX.X))
                ts(nmax[:, 0:1], rsum[:, 0:1], -SCALE_B, None, ALU.mult).then_inc(biased, 1)

            def norm_b(i, c):
                dve.wait_ge(exp_done, 8 * i + (5 + c))
                link(nc.vector.reciprocal(rsum[:, 0:1], sums[:, 0:1]))
                ts(pr[:, :], sc[:, 0:6 * P], rsum[:, 0:1], None, ALU.mult).then_inc(p_ready, 1)

            def turned(i, idx, hi_part, dst, n):
                dve.wait_ge(t_hi, 16 * i + (idx + 1))
                tt(dst, tr_ps[idx % 2][:, 0:n * P].rearrange("p (n q) -> p n q", n=n), hi_part.bitcast(f32),
                   ALU.subtract).then_inc(t_free, 1)

            def split_block(i, w):
                dve.wait_ge(qh_done, 8 * i + (SPLIT.index(w) + 1))
                tt(qk_lo[w][:, :], blk[w][:, :], qk_hi[w][:, :].bitcast(f32), ALU.subtract).then_inc(ql_done, 1)

            def silu(i, idx, w):
                dve.wait_ge(th_ready, 3 * i + (idx + 1))
                link(stt(blk[w][:, :], th[:, :], 1.0, blk[w][:, :], ALU.add, ALU.mult))

            first_turn = [5, 8, 11, 14]
            STEPS1 = 2 + 4 + 12 + 4 + 4 + 3 + 2 + 5
            with dve.Fori(0, HEADS) as i:
                enter(i, STEPS1)
                link(nc.vector.tensor_copy(slope[:, :], slopes[:, bass.ds(4 * i, 4)]))
                link(nc.vector.tensor_copy(taps[:, :], cols[:, bass.ds(3 * i + S_CONV, 3)]))
                for w in range(NBLK1):
                    split_1(i, 2 * w)
                    if 3 <= w < 7:
                        norm_a(i, w - 3)
                    if w == 4:
                        silu(i, 0, AZ)
                    if 11 <= w < 15:
                        norm_b(i, w - 11)
                    if 12 <= w < 15:
                        turned(i, first_turn[w - 12] + 2, v_hi[w - 12][:, :, :], v_lo[w - 12][:, :, :], 4)
                    if w == 14:
                        silu(i, 1, BZ)
                    if w == 9:
                        dve.wait_ge(sd_ready, i + 1)
                        link(nc.vector.reciprocal(inv_a[:, :], inv_a[:, :]))
                        link(stt(o_a[:, :], o_a[:, :], gsub[:, :], inv_a[:, :], ALU.mult, ALU.mult))
                        dve.wait_ge(y_stored[0], 16 * i + 16)
                        stt(y_a[:, :], o_a[:, :], 0.5, blk[AZ][:, :], ALU.mult, ALU.mult).then_inc(y_ready, 1)
                    scale_block(i, w)
                    split_1(i, 2 * w + 1)
                    if w in SPLIT:
                        split_block(i, w)
                    if 2 <= w < 6:
                        bias_a(i, w - 2)
                    if 10 <= w < 14:
                        bias_b(i, w - 10)
                    if w == 3:
                        turned(i, 0, v_hi[0][:, :, :], v_lo[0][:, :, :], 4)
                    if 3 <= w < 7:
                        q = w - 3
                        turned(i, 1 + q, *[t[:, 0:q + 1, q * P:(q + 1) * P] for t in pt_a], q + 1)
                    if 11 <= w < 15:
                        c = w - 11
                        turned(i, first_turn[c], *[t[:, 0:4, c, :] for t in pt_b], 4)
                        turned(i, first_turn[c] + 1, *[t[:, 4:6, c, :] for t in pt_b], 2)
                    if w == 7:
                        dve.wait_ge(o_ready, 2 * i + 1)
                        nc.vector.tensor_copy(o_a[:, :], o_ps[:, :]).then_inc(o_free, 1)
                    if w == 8:
                        dve.wait_ge(s_ready, 9 * i + 5)
                        ts(sq_a[:, :], sc_ps[0][:, :], 1.0 / P, EPS, ALU.mult, ALU.add).then_inc(s_free, 1)
                    if w == 15:
                        dve.wait_ge(o_ready, 2 * i + 2)
                        dve.wait_ge(y_stored[1], 16 * i + 16)
                        dve.wait_ge(y_stored[2], 16 * i + 16)
                        stt(y_b[:, :].rearrange("p (b c) -> p b c", c=4), o_ps[:, :].rearrange("p (c b) -> p b c", c=4), 0.5,
                            blk[BZ][:, :].rearrange("p (b c) -> p b c", c=4), ALU.mult, ALU.mult).then_inc(o_free, 1)
                    if w == CX:
                        dve.wait_ge(evac_done, NBLK1 * i + (RING + CX + 1))
                        link(tt(u[:, 2:T + 2], blk[CC][:, :], blk[CX][:, :], ALU.mult))
                        link(ts(blk[CC][:, :], u[:, 2:T + 2], taps[:, 2:3], None, ALU.mult))
                        link(stt(blk[CC][:, :], u[:, 1:T + 1], taps[:, 1:2], blk[CC][:, :], ALU.mult, ALU.add))
                        link(stt(blk[CC][:, :], u[:, 0:T], taps[:, 0:1], blk[CC][:, :], ALU.mult, ALU.add))
                        link(tt(blk[CC][:, :], blk[CC][:, :], blk[CB][:, :], ALU.mult))
                    if w == CZ:
                        silu(i, 2, CZ)
                        dve.wait_ge(y_stored[2], 16 * i + 16)
                        dve.wait_ge(y_stored[1], 16 * i + 32)
                        stt(y_c[:, :], blk[CC][:, :], 0.5, blk[CZ][:, :], ALU.mult, ALU.mult).then_inc(y_ready, 1)
                leave(HEADS)

            def merge(j, t, used, gates):
                if t in (1, 3, 5):
                    b = t // 2
                    dve.wait_ge(pe_used, used)
                    tt(gate[b][:, :], pb[b][:, :], rstd[:, :], ALU.mult).then_inc(evac_done, 1)
                if t >= 6:
                    b = t - 6
                    dve.wait_ge(pe_used, used)
                    dve.wait_ge(gate_done, gates)
                    stt(gate[b][:, :], gate[b][:, :], 1.0, pb[b][:, :], ALU.add, ALU.mult).then_inc(evac_done, 1)
                    if b == 1:
                        dve.wait_ge(evac_done, NBLK2 * j + (NBLK1 * HEADS + RING + 5))
                        link(tt(gate[0][:, :], gate[0][:, :], gate[1][:, :], ALU.add))
                    if b == 2:
                        dve.wait_ge(evac_done, NBLK2 * j + (NBLK1 * HEADS + RING + 6))
                        dve.wait_ge(m_stored, 16 * j + 16)
                        tt(merged[:, :], gate[0][:, :], gate[2][:, :], ALU.add).then_inc(m_ready, 1)

            n_last = W1 + (KT - 1) * NHU2
            r = W1 + RING
            for t, tick in enumerate(first_merged_ring()):
                for n_item, (kind, n) in enumerate(tick):
                    if kind == "y":
                        split_lo_pair(r % RING, y_lo, y_hi, n, r + 1)
                    else:
                        split_lo(r % RING, n % RING, r + 1)
                    r += 1
                merge(0, t, W1 + RING + t + 1, 3)
            with dve.Fori(1, KT - 1) as j:
                enter(j - 1, 1)
                for t in range(NHU2):
                    split_lo(t % RING, t % RING, NHU2 * j + (W1 + N_Y + RING + t + 1))
                    merge(j, t, NHU2 * j + (W1 + RING + t + 1), 3 * j + 3)
                leave(KT - 2)
            r = R_LAST
            for t, tick in enumerate(last_merged_ring()):
                for kind, n in tick:
                    if kind == "w":
                        split_lo(r % RING, n % RING, r + 1)
                    elif n < N_M - 1:
                        split_lo_pair(r % RING, act_lo, act_hi, n, r + 1)
                    else:
                        dve.wait_ge(hi_done, r + 1)
                        tt(act_lo[:, KT - 2, :], raw[r % RING][:, 0:T], act_hi[:, KT - 2, :].bitcast(f32),
                           ALU.subtract).then_inc(lo_done, 1)
                    r += 1
                merge(KT - 1, t, n_last + RING + t + 1, 3 * KT)
            dve.wait_ge(m15_hi, 1)
            tt(act_lo[:, KT - 1, :], merged[:, :], act_hi[:, KT - 1, :].bitcast(f32), ALU.subtract).then_inc(m15_lo, 1)
            r, n = R_OUT, W1 + W2 + RING

            def add_residual(used, bank, blk_i):
                dve.wait_ge(pe_used, used)
                x_i = res[:, blk_i, :] if isinstance(blk_i, int) else res[:, bass.ds(blk_i, 1), :].rearrange("p o q -> p (o q)")
                stt(x_i, pb[bank][:, :], 0.5, x_i, ALU.mult, ALU.add).then_inc(evac_done, 1)

            for t in range(2):
                split_lo((r + t) % RING, (n + t) % RING, r + t + 1)
            dve.wait_ge(res_in, 16)
            add_residual(n + 2, 0, 0)

            def out_round(m, splits):
                for s in range(3):
                    for half in range(2):
                        t = 2 * s + half
                        if t < splits:
                            split_lo((r + 2 + t) % RING, (n + 2 + t) % RING, 6 * m + (r + 2 + t + 1))
                    add_residual(6 * m + (n + 2 + 2 * s + 2), (1 + s) % RING, 3 * m + (1 + s))

            with dve.Fori(0, 4) as m:
                out_round(m, 6)
            out_round(4, 3)
            dve.wait_ge(std_done, 2)
            nc.vector.reciprocal(fcol[:, :], fcol[:, :]).then_inc(fcol_done, 1)
            dve.wait_ge(frstd_done, 1)
            for k in BY_VECTOR:
                tt(res[:, k, :], res[:, k, :], frstd[:, :], ALU.mult).then_inc(fin_ready, 1)


def kernel(**inputs):
    import numpy as np
    import concourse.bacc as bacc
    from concourse.bass_utils import run_bass_kernel_spmd

    def get(name):
        return np.ascontiguousarray(inputs[name])

    const = np.zeros((P, C_END), np.float32)
    p = np.arange(P)[:, None]
    dist = p + (T - P) - np.arange(T)[None, :]
    const[:, C_MA:C_MA + T] = np.where(dist >= 0, dist, FAR)
    dist = 4 * p + 3 - np.arange(515)[None, :]
    const[:, C_M0:C_M0 + 515] = np.where((dist >= 0) & (dist <= 128), dist, FAR)
    dist = 4 * (p - np.arange(P)[None, :])
    const[:, C_M12:C_M12 + P] = np.where(dist >= 0, dist, FAR)
    const[:, C_M12 + P:C_M12 + 2 * P] = np.where((dist >= 0) & (dist % 16 == 0), dist, FAR)
    const[:, C_ID:C_ID + P] = np.eye(P)
    const[:, C_ONE:C_ONE + P] = 1.0
    slopes = 2.0 ** (-8.0 * np.arange(1, 4 * HEADS + 1) / (4 * HEADS))
    for h in range(HEADS):
        const[:, C_SL + 4 * h] = -slopes[h] / SCALE_A
        for g in range(3):
            const[:, C_SL + 4 * h + 1 + g] = -slopes[HEADS + g * HEADS + h] / SCALE_B

    def units(w, half):
        return w[half * 8 * P:(half + 1) * 8 * P].reshape(8, P, -1, P).transpose(2, 1, 0, 3).reshape(-1, P, HU)

    w_in = get("w_in")[0]
    wi = [units(w_in, half) for half in range(2)]
    wb = [units(get(f"w_branch_{x}")[0], 0) for x in "abc"]
    wo = [units(get("w_out")[0], half) for half in range(2)]
    nb = HEADS
    order = [0, nb, 2 * nb, 3 * nb]
    b0 = 4 * nb
    order += [b0, b0 + nb, b0 + 3 * nb, b0 + 4 * nb, b0 + 6 * nb, b0 + 7 * nb]
    order += [b0 + 2 * nb, b0 + 5 * nb, b0 + 8 * nb, b0 + 9 * nb]
    c0 = b0 + 10 * nb
    order += [c0, c0 + nb, c0 + 2 * nb, c0 + 3 * nb]
    g0 = c0 + 4 * nb
    wst = np.empty((W1 + W2 + W3, P, HU), np.float32)
    n = 0
    for h in range(HEADS):
        for b in order:
            for half in range(2):
                wst[n] = wi[half][b + h]
                n += 1
    for j in range(KT):
        for b in range(3):
            for half in range(2):
                wst[n] = wi[half][g0 + b * KT + j]
                n += 1
        for b in range(3):
            wst[n] = wb[b][j]
            n += 1
    for j in range(NBLK3):
        for half in range(2):
            wst[n] = wo[half][j]
            n += 1

    x_t = np.ascontiguousarray(get("x")[0].T).reshape(KT, P, T)
    cols = np.concatenate([
        get("norm_g")[0].reshape(KT, P).T,
        get("gate_b")[0].reshape(3, KT, P).transpose(2, 1, 0).reshape(P, 48),
        get("subln_g")[0].reshape(P, 1),
        get("conv_w")[0].reshape(3, HEADS, P).transpose(2, 1, 0).reshape(P, 24),
        get("final_g").reshape(KT, P).T], axis=1)
    lam = np.stack([get(f"lambda_{x}")[0] for x in ("q1", "k1", "q2", "k2")]).reshape(1, 256)
    arrays = {"wst": wst, "x_t": x_t, "cols_d": np.ascontiguousarray(cols), "lam_d": lam, "const_d": const}

    nc = bacc.Bacc("TRN2", target_bir_lowering=False, num_devices=1)
    args = [nc.dram_tensor(k, a.shape, mybir.dt.from_np(a.dtype), kind="ExternalInput").ap() for k, a in arrays.items()]
    args.append(nc.dram_tensor("out_0", (KT, P, T), mybir.dt.float32, kind="ExternalOutput").ap())
    program(nc, *args)
    r = run_bass_kernel_spmd(nc, [arrays], core_ids=[0])
    return r.results[0]["out_0"].reshape(D, T).T.reshape(1, T, D)
```

```python
import math
from contextlib import ExitStack

import concourse.bass as bass
from concourse import mybir

P = 128
D = 2048
T = 512
KT = D // P
HEADS = 8
HU = 8 * P
RING = 3
NBLK1, NBLK2, NBLK3 = 18, 6, 16
NHU1, NHU2 = 36, 9
W1 = HEADS * NHU1
W2 = KT * NHU2
W3 = 2 * NBLK3
LAM_INIT = 0.8 - 0.6 * math.exp(-0.3 * 0)
EPS = 1e-6
FAR = 1e30
SCALE_A = 64 ** -0.5
SCALE_B = 128 ** -0.5
C_MA, C_M0, C_M12, C_ID, C_ONE, C_SL = 0, 512, 512 + 515, 1283, 1283 + 128, 1283 + 256
C_END = C_SL + 4 * HEADS
S_G, S_GB, S_SUB, S_CONV, S_FG = 0, 16, 64, 65, 89
S_END = 105
Y_ITEMS = [1, 2, 2, 2, 2, 2, 1, 0, 0]
M_ITEMS = [0, 0, 0, 0, 2, 2, 1, 2, 1]
N_Y, N_M = 12, 8
AQ, AK, AV, AZ, Q0, K0, Q1, K1, Q2, K2, V0, V1, V2, BZ, CB, CC, CX, CZ = range(NBLK1)


def first_merged_ring():
    ticks, y = [], 0
    for t in range(NHU2):
        items = [("y", y + m) for m in range(Y_ITEMS[t])]
        y += Y_ITEMS[t]
        ticks.append(items + [("w", W1 + RING + t)])
    return ticks


def last_merged_ring():
    ticks, m = [], 0
    for t in range(NHU2):
        ticks.append([("w", W1 + (KT - 1) * NHU2 + RING + t)] + [("m", m + x) for x in range(M_ITEMS[t])])
        m += M_ITEMS[t]
    return ticks


R_FIRST = W1 + RING
R_LAST = W1 + N_Y + (KT - 1) * NHU2 + RING
PLACE = {x: R_FIRST + n for n, x in enumerate(x for tick in first_merged_ring() for x in tick)}
PLACE |= {x: R_LAST + n for n, x in enumerate(x for tick in last_merged_ring() for x in tick)}
R_OUT = R_LAST + NHU2 + N_M
SPLIT = [AQ, AK, Q0, K0]
STAGED = SPLIT + [AV, V0, V1, V2]
TURN_P, TURN_V = [5, 8, 11, 14], [7, 10, 13]
TURN_SPLIT = [0, 1, 2, 3, 4, 5, 7, 8, 11, 14]
SPLIT_AT = (0, 8, 10)
FIRST_UNITS = [(0, 0), (1, 0), (0, 1), (1, 1)]
X_LOADS = [(0, 1), (1, 1)] + [(k, 2) for k in range(2, KT, 2)]
SQ_VECTOR, SQ_SCALAR = [9, 10], list(range(11, KT))
SQ_POOL = [k for k in range(KT) if k not in SQ_VECTOR + SQ_SCALAR]
X_ADDS = len(SQ_VECTOR + SQ_SCALAR)
BY_POOL = [3, 7, 11, 15]
BY_VECTOR = [k for k in range(KT) if k not in BY_POOL]


def program(nc, wst, x_t, cols_d, lam_d, const_d, out_d):
    f32, f32r = mybir.dt.float32, mybir.dt.float32r
    ALU, ACT, AX = mybir.AluOpType, mybir.ActivationFunctionType, mybir.AxisListType
    y_dram = nc.dram_tensor("y_dram", (3 * HEADS, P, T), f32, kind="Internal").ap()
    m_dram = nc.dram_tensor("m_dram", (KT, P, T), f32, kind="Internal").ap()

    with ExitStack() as ctx:
        def sb_in(c):
            return lambda name, shape, dt=f32: c.enter_context(nc.sbuf_tensor(name, shape, dt))

        def sem(name):
            return ctx.enter_context(nc.semaphore(name))

        sb = sb_in(ctx)
        act_hi, act_lo = sb("act_hi", [P, KT, T], f32r), sb("act_lo", [P, KT, T], f32r)
        raw = [sb(f"raw{i}", [P, HU]) for i in range(RING)]
        w_hi = [sb(f"w_hi{i}", [P, HU], f32r) for i in range(RING)]
        w_lo = [sb(f"w_lo{i}", [P, HU], f32r) for i in range(RING)]
        rstd = sb("rstd", [P, T])
        cols = sb("cols", [P, S_END])
        eps = sb("eps", [P, 1])
        lam_col = sb("lam_col", [P, 1])
        gsub = sb("gsub", [P, 1])
        ones = sb("ones", [P, P])
        ident = sb("ident", [P, P])

        with ExitStack() as c1:
            s1 = sb_in(c1)
            y_b, y_a = s1("y_b", [P, T]), s1("y_a", [P, T])
            y_c = y_b
            masks = s1("masks", [P, C_ID])
            slopes = s1("slopes", [P, 4 * HEADS])
            slope = s1("slope", [P, 4])
            taps = s1("taps", [P, 3])
            lam_in = s1("lam_in", [1, 4 * 64])
            lam_w = s1("lam_w", [1, 2 * 64])
            lam_s = s1("lam_s", [1, 8])
            nmax, sums, rsum = s1("nmax", [P, 2]), s1("sums", [P, 2]), s1("rsum", [P, 2])
            small_words = 2 * T + C_ID + 4 * HEADS + 7 + 6 * 64 + 8 + 6 + 64
            stage = [s1(f"stage{n}", [P, T]) for n in range(2)]
            z = s1("z", [P, T])
            cb, cc, cx = s1("cb", [P, T]), s1("cc", [P, T]), s1("cx", [P, T])
            blk = {b: stage[b % 2] for b in STAGED} | {AZ: z, BZ: z, CZ: z, CB: cb, CC: cc, CX: cx}
            for b in (Q1, K1, Q2, K2):
                blk[b] = s1(f"qk{b}", [P, T])
            qk_hi = {b: s1(f"qk_hi{b}", [P, T], f32r) for b in SPLIT}
            qk_lo = {b: s1(f"qk_lo{b}", [P, T], f32r) for b in SPLIT}
            v_hi, v_lo = s1("v_hi", [P, 4, P], f32r), s1("v_lo", [P, 4, P], f32r)
            v_g = {g: s1(f"v_g{g}", [P, 4, P]) for g in (1, 2)}
            pt_hi, pt_lo = s1("pt_hi", [P, 16 * P], f32r), s1("pt_lo", [P, 16 * P], f32r)
            pt_g = s1("pt_g", [P, 2, 4, P])
            sq_hi, sq_lo = s1("sq_hi", [P, T], f32r), s1("sq_lo", [P, T], f32r)
            ones_r = s1("ones_r", [P, P], f32r)
            th, tmp_a, o_a = s1("th", [P, T]), s1("tmp_a", [P, T]), s1("o_a", [P, T])
            sq_a, inv_a = th, tmp_a
            sc, pr = s1("sc", [P, 2 * T]), s1("pr", [P, 6 * P])
            u = s1("u", [P, T + 2])
            sc_a = sc[:, :].rearrange("p (m q) -> p m q", m=2)
            pt_a = [t[:, :].rearrange("p (n q) -> p n q", n=4) for t in (pt_hi, pt_lo)]
            pt_b = [t[:, :].rearrange("p (n c b) -> p n c b", n=4, c=4) for t in (pt_hi, pt_lo)]
        with ExitStack() as c0:
            s0 = sb_in(c0)
            s0("below", [P, small_words])
            x_raw = s0("x_raw", [P, KT, T])
            xacc, xacc_pool = s0("xacc", [P, T]), s0("xacc_pool", [P, T])
        with ExitStack() as c2:
            s2 = sb_in(c2)
            gate = [s2(f"gate{b}", [P, T]) for b in range(3)]
            merged = s2("merged", [P, T])
            y_hi, y_lo = s2("y_hi", [P, 3 * HEADS, T], f32r), s2("y_lo", [P, 3 * HEADS, T], f32r)
        with ExitStack() as c3:
            s3 = sb_in(c3)
            s3("kept", [P, 4 * T])
            res = s3("res", [P, KT, T])
            rsq = [s3(f"rsq{i}", [P, T]) for i in range(RING)]
            racc = s3("racc", [P, T])
            frstd = s3("frstd", [P, T])
            fcol = s3("fcol", [P, 4])

        pb = [ctx.enter_context(nc.psum_tensor(f"proj{i}", [P, T], f32)) for i in range(RING)]
        sc_ps = [ctx.enter_context(nc.psum_tensor(f"sc_ps{i}", [P, T], f32)) for i in range(2)]
        tr_ps = [ctx.enter_context(nc.psum_tensor(f"tr_ps{i}", [P, T], f32)) for i in range(2)]
        o_ps = ctx.enter_context(nc.psum_tensor("o_ps", [P, T], f32))

        cols_in, lam_ones_in, const_in = sem("cols_in"), sem("lam_ones_in"), sem("const_in")
        x_in = [sem(f"x_in{i}") for i in range(len(X_LOADS))]
        res_in = sem("res_in")
        raw_in = [sem(f"raw_in{i}") for i in range(RING)]
        y_stored = [sem(f"y_stored{b}") for b in range(3)]
        m_stored = sem("m_stored")
        out_stored = sem("out_stored")
        hi_done, lo_done, pe_used = sem("hi_done"), sem("lo_done"), sem("pe_used")
        evac_done = sem("evac_done")
        xh_done, xl_done = sem("xh_done"), sem("xl_done")
        xsq_done, xacc_add, ss_done, std_done = sem("xsq_done"), sem("xacc_add"), sem("ss_done"), sem("std_done")
        pool_sq, pool_add = sem("pool_sq"), sem("pool_add")
        sq_split = sem("sq_split")
        qh_done, ql_done, t_hi = sem("qh_done"), sem("ql_done"), sem("t_hi")
        m15_hi, m15_lo = sem("m15_hi"), sem("m15_lo")
        lam_sum, lam_exp, lam_set, lam_bc = sem("lam_sum"), sem("lam_exp"), sem("lam_set"), sem("lam_bc")
        s_ready, s_free = sem("s_ready"), sem("s_free")
        t_ready, t_free = sem("t_ready"), sem("t_free")
        o_ready, o_free = sem("o_ready"), sem("o_free")
        biased, exp_done, p_ready = sem("biased"), sem("exp_done"), sem("p_ready")
        th_ready, sq_ready, sd_ready, y_ready = sem("th_ready"), sem("sq_ready"), sem("sd_ready"), sem("y_ready")
        gate_done, m_ready = sem("gate_done"), sem("m_ready")
        rsq_done, racc_done, rg_done = sem("rsq_done"), sem("racc_done"), sem("rg_done")
        fcol_done, frstd_ps, frstd_done, fin_ready = sem("fcol_done"), sem("frstd_ps"), sem("frstd_done"), sem("fin_ready")
        fin_pool = sem("fin_pool")
        dve_step = sem("dve_step")

        block = ctx.enter_context(nc.Block())

        def natural(ap):
            return ap

        def by_class(ap):
            return ap.rearrange("p (b c) -> p c b", c=4)

        def as_class(ap):
            return ap.rearrange("p (c b) -> p c b", c=4)

        @block.sync
        def _(sp):
            def load_w(slot, n):
                src = wst[n, :, :] if isinstance(n, int) else wst[bass.ds(n, 1), :, :].rearrange("o p f -> p (o f)")
                sp.dma_start(raw[slot][:, :], src).then_inc(raw_in[slot], 16)

            def load_pair(slot, dram, item):
                sp.dma_start(raw[slot][:, :].rearrange("p (t q) -> p t q", t=2),
                             dram[2 * item:2 * item + 2, :, :].rearrange("t p q -> p t q")).then_inc(raw_in[slot], 16)

            sp.dma_start(cols[:, :], cols_d).then_inc(cols_in, 16)
            for g, (k, n) in enumerate(X_LOADS):
                if k in SPLIT_AT:
                    load_w(SPLIT_AT.index(k), SPLIT_AT.index(k))
                sp.dma_start(x_raw[:, k:k + n, :], x_t[k:k + n, :, :].rearrange("k p t -> p k t")).then_inc(x_in[g], 16)
            sp.dma_start(masks[:, :], const_d[:, 0:C_ID]).then_inc(const_in, 16)
            sp.dma_start(ident[:, :], const_d[:, C_ID:C_ID + P]).then_inc(const_in, 16)
            sp.dma_start(slopes[:, :], const_d[:, C_SL:C_END]).then_inc(const_in, 16)
            with sp.Fori(1, W1 // RING + 1) as i:
                for s in range(RING):
                    sp.wait_ge(lo_done, RING * i + s - RING + 1)
                    load_w(s, RING * i + s)
            for b in range(2):
                sp.wait_ge(y_stored[b], 16 * (HEADS + 1))
            r = W1 + RING
            for kind, n in [x for tick in first_merged_ring() for x in tick]:
                sp.wait_ge(lo_done, r - RING + 1)
                if kind == "y":
                    if n == N_Y - 1:
                        sp.wait_ge(y_stored[2], 16 * (HEADS + 1))
                    load_pair(r % RING, y_dram, n)
                else:
                    load_w(r % RING, n)
                r += 1
            n0 = W1 + NHU2 + RING
            with sp.Fori(0, (KT - 2) * NHU2 // RING) as i:
                for s in range(RING):
                    sp.wait_ge(lo_done, RING * i + (r + s - RING + 1))
                    load_w((r + s) % RING, RING * i + (n0 + s))
            r += (KT - 2) * NHU2
            for kind, n in [x for tick in last_merged_ring() for x in tick]:
                sp.wait_ge(lo_done, r - RING + 1)
                if kind == "m" and n < N_M - 1:
                    sp.wait_ge(m_stored, 16 * (2 * n + 3))
                    load_pair(r % RING, m_dram, n)
                elif kind == "m":
                    sp.wait_ge(m_stored, 16 * KT)
                    sp.dma_start(raw[r % RING][:, 0:T], m_dram[KT - 2, :, :]).then_inc(raw_in[r % RING], 16)
                else:
                    load_w(r % RING, n)
                r += 1
            n0 = W1 + W2 + RING
            left = W3 - RING
            with sp.Fori(0, left // RING) as i:
                for s in range(RING):
                    sp.wait_ge(lo_done, RING * i + (r + s - RING + 1))
                    load_w((r + s) % RING, RING * i + (n0 + s))
            for s in range(left - left % RING, left):
                sp.wait_ge(lo_done, r + s - RING + 1)
                load_w((r + s) % RING, n0 + s)

            for n, k in enumerate(BY_POOL):
                sp.wait_ge(fin_pool, n + 1)
                sp.dma_start(out_d[k, :, :], res[:, k, :]).then_inc(out_stored, 16)
            sp.wait_ge(out_stored, 16 * KT)

        @block.gpsimd
        def _(pool):
            for n, k in enumerate(SQ_POOL):
                pool.wait_ge(xl_done, k + 1)
                dst = xacc_pool[:, :] if n == 0 else x_raw[:, k, :]
                nc.gpsimd.tensor_tensor(dst, x_raw[:, k, :], x_raw[:, k, :], ALU.mult).then_inc(pool_sq, 1)
                if n:
                    pool.wait_ge(pool_sq, n + 1)
                    if n > 1:
                        pool.wait_ge(pool_add, n - 1)
                    nc.gpsimd.tensor_tensor(xacc_pool[:, :], xacc_pool[:, :], x_raw[:, k, :], ALU.add).then_inc(pool_add, 1)
            pool.wait_ge(rsq_done, 1)
            nc.gpsimd.tensor_copy(racc[:, :], rsq[0][:, :]).then_inc(racc_done, 1)

            def add_squares(m, s):
                pool.wait_ge(rsq_done, 3 * m + (2 + s))
                pool.wait_ge(racc_done, 3 * m + (1 + s))
                nc.gpsimd.tensor_tensor(racc[:, :], racc[:, :], rsq[(1 + s) % RING][:, :], ALU.add).then_inc(racc_done, 1)

            with pool.Fori(0, 4) as m:
                for s in range(3):
                    add_squares(m, s)
            for s in range(2):
                add_squares(4, s)
            pool.wait_ge(frstd_done, 1)
            for k in BY_POOL:
                nc.gpsimd.tensor_tensor(res[:, k, :], res[:, k, :], frstd[:, :], ALU.mult).then_inc(fin_pool, 1)

        @block.tensor
        def _(pe):
            pe.sem_inc(pe_used, RING)

            def three(out, w_h, w_l, a_h, a_l, first, last):
                nc.tensor.matmul(out, w_h, a_h, start=first, stop=False)
                nc.tensor.matmul(out, w_h, a_l, start=False, stop=False)
                return nc.tensor.matmul(out, w_l, a_h, start=False, stop=last)

            def multiply(bank, slot, m_hi, m_lo, k0, first, last, fresh=False):
                for k in range(8):
                    if fresh:
                        pe.wait_ge(xl_done, k0 + k + 1)
                    ws = slice(k * P, (k + 1) * P)
                    end = three(pb[bank][:, :], w_hi[slot][:, ws], w_lo[slot][:, ws], m_hi[:, k0 + k, :],
                                m_lo[:, k0 + k, :], first and k == 0, last and k == 7)
                end.then_inc(pe_used, 1)

            def scaled(i, b):
                pe.wait_ge(evac_done, NBLK1 * i + (RING + b + 1))

            def split_ready(i, b):
                pe.wait_ge(ql_done, len(SPLIT) * i + (SPLIT.index(b) + 1))

            def scores_a(i, q):
                n = P * (q + 1)
                split_ready(i, AK)
                pe.wait_ge(s_free, 9 * i + (q + 1))
                for step, (q_part, k_part) in enumerate(((qk_hi, qk_hi), (qk_hi, qk_lo), (qk_lo, qk_hi))):
                    for m in range(2):
                        rows, qs = slice(64 * m, 64 * m + 64), slice(P * q, P * q + P)
                        end = nc.tensor.matmul(sc_ps[m][:, 0:n], q_part[AQ][rows, qs], k_part[AK][rows, 0:n],
                                               start=step == 0, stop=step == 2)
                end.then_inc(s_ready, 1)

            def turn(i, idx, tiles):
                pe.wait_ge(t_free, 16 * i + (idx + 1))
                for n, tile in enumerate(tiles):
                    end = nc.tensor.transpose(tr_ps[idx % 2][:, n * P:(n + 1) * P], tile, ident[:, :])
                end.then_inc(t_ready, 1)

            def probs_a(i, q):
                pe.wait_ge(p_ready, 8 * i + (q + 1))
                turn(i, 1 + q, [pr[:, n * P:(n + 1) * P] for n in range(q + 1)])

            def values_a(i):
                pe.wait_ge(t_free, 16 * i + (2 + 5))
                pe.wait_ge(o_free, 2 * i + 1)
                for n in range(4):
                    end = three(o_ps[:, n * P:T], v_hi[:, n, :], v_lo[:, n, :], pt_a[0][:, n, n * P:T],
                                pt_a[1][:, n, n * P:T], n == 0, n == 3)
                end.then_inc(o_ready, 1)

            def squares_a(i):
                pe.wait_ge(sq_split, i + 1)
                pe.wait_ge(s_free, 9 * i + 5)
                nc.tensor.matmul(sc_ps[0][:, :], ones_r[:, :], sq_hi[:, :], start=True, stop=False)
                nc.tensor.matmul(sc_ps[0][:, :], ones_r[:, :], sq_lo[:, :], start=False, stop=True).then_inc(s_ready, 1)

            def scores_b(i, c):
                scaled(i, K2)
                pe.wait_ge(s_free, 9 * i + (6 + c))
                qs = slice(c * P, (c + 1) * P)
                for g, (q, k) in enumerate(((Q0, K0), (Q1, K1), (Q2, K2))):
                    if g == 0:
                        three(sc_ps[0][:, :], qk_hi[q][:, qs], qk_lo[q][:, qs], qk_hi[k][:, :], qk_lo[k][:, :], True, True)
                    else:
                        end = nc.tensor.matmul(sc_ps[1][:, (g - 1) * P:g * P], blk[q][:, qs], blk[k][:, qs],
                                               start=True, stop=True)
                end.then_inc(s_ready, 1)

            def probs_b(i, c):
                pe.wait_ge(p_ready, 8 * i + (5 + c))
                turn(i, TURN_P[c], [pr[:, n * P:(n + 1) * P] for n in range(4)])
                turn(i, TURN_P[c] + 1, [pr[:, n * P:(n + 1) * P] for n in range(4, 6)])

            def values_b(i):
                pe.wait_ge(t_free, 16 * i + (2 + 16))
                pe.wait_ge(o_free, 2 * i + 2)
                for g in (1, 2):
                    for c in range(4):
                        nc.tensor.matmul(o_ps[:, c * P:(c + 1) * P], v_g[g][:, c, :], pt_g[:, g - 1, c, :],
                                         start=g == 1 and c == 0, stop=False)
                for n in range(4):
                    bs = slice(32 * n, min(32 * n + 64, P))
                    end = three(as_class(o_ps[:, :])[:, :, bs], v_hi[:, n, :], v_lo[:, n, :], pt_b[0][:, n, :, bs],
                                pt_b[1][:, n, :, bs], False, n == 3)
                end.then_inc(o_ready, 1)

            def quarter(tile):
                return [tile[:, n * P:(n + 1) * P] for n in range(4)]

            def first_blocks():
                for n, (w, half) in enumerate(FIRST_UNITS):
                    pe.wait_ge(evac_done, w + 1)
                    pe.wait_ge(lo_done, n + 1)
                    multiply(w, n % RING, act_hi, act_lo, 8 * half, half == 0, half == 1, fresh=w == 0)
                pe.wait_ge(lam_ones_in, 16 * 2)
                pe.wait_ge(xacc_add, X_ADDS)
                nc.tensor.matmul(o_ps[:, :], ones[:, :], xacc[:, :], start=True, stop=True).then_inc(ss_done, 1)
                pe.wait_ge(lam_set, 1)
                pe.wait_ge(const_in, 16 * 3)
                nc.tensor.matmul(tr_ps[0][:, 0:1], ones[0:1, :], lam_s[0:1, 4:5], start=True,
                                 stop=True).then_inc(lam_bc, 1)

            def blocks(i, first):
                for w in range(first, NBLK1):
                    pe.wait_ge(evac_done, NBLK1 * i + (w + 1))
                    pe.wait_ge(lo_done, NHU1 * i + (2 * w + 1))
                    multiply(w % RING, 2 * w % RING, act_hi, act_lo, 0, True, False)
                    if w == 12:
                        scaled(i, V0)
                        turn(i, 7, quarter(blk[V0]))
                    if w == 13:
                        scaled(i, V1)
                        turn(i, 10, quarter(blk[V1]))
                    if w == 14:
                        scaled(i, V2)
                        turn(i, 13, quarter(blk[V2]))
                    pe.wait_ge(lo_done, NHU1 * i + (2 * w + 2))
                    multiply(w % RING, (2 * w + 1) % RING, act_hi, act_lo, 8, False, True)
                    if 2 <= w < 6:
                        scores_a(i, w - 2)
                    if w == 3:
                        scaled(i, AV)
                        turn(i, 0, quarter(blk[AV]))
                    if 3 <= w < 7:
                        probs_a(i, w - 3)
                    if w == 7:
                        values_a(i)
                    if w == 8:
                        squares_a(i)
                    if 10 <= w < 14:
                        scores_b(i, w - 10)
                    if 11 <= w < 15:
                        probs_b(i, w - 11)
                    if w == 15:
                        values_b(i)

            first_blocks()
            blocks(0, 2)
            with pe.Fori(1, HEADS) as i:
                blocks(i, 0)

            def merge_block(evac, ready, y_needed=(0, 0, 0)):
                for b in range(3):
                    pe.wait_ge(evac_done, evac + (b + 1))
                    for half in range(2):
                        pe.wait_ge(lo_done, ready[2 * b + half])
                        multiply(b, (2 * b + half) % RING, act_hi, act_lo, 8 * half, half == 0, half == 1)
                for b in range(3):
                    pe.wait_ge(evac_done, evac + (b + 4))
                    pe.wait_ge(lo_done, ready[6 + b])
                    if y_needed[b]:
                        pe.wait_ge(lo_done, y_needed[b])
                    multiply(b, (6 + b) % RING, y_hi, y_lo, 8 * b, True, True)

            evac0 = NBLK1 * HEADS
            merge_block(evac0, [W1 + t + 1 if t < RING else PLACE["w", W1 + t] + 1 for t in range(NHU2)],
                        [PLACE["y", 4 * b + 3] + 1 for b in range(3)])
            with pe.Fori(1, KT - 1) as j:
                merge_block(NBLK2 * j + evac0, [NHU2 * j + (W1 + N_Y + t + 1) for t in range(NHU2)])
            n_last = W1 + (KT - 1) * NHU2
            merge_block(NBLK2 * (KT - 1) + evac0,
                        [n_last + N_Y + t + 1 if t < RING else PLACE["w", n_last + t] + 1 for t in range(NHU2)])

            evac0 += NBLK2 * KT
            n0 = W1 + W2

            def out_block(bank, slot, evac, ready):
                pe.wait_ge(evac_done, evac + 1)
                for half in range(2):
                    for sem_, value in ready[half]:
                        pe.wait_ge(sem_, value)
                    multiply(bank, (slot + half) % RING, act_hi, act_lo, 8 * half, half == 0, half == 1)

            out_block(0, 0, evac0, [[(lo_done, PLACE["w", n0] + 1), (lo_done, PLACE["m", 3] + 1)],
                                    [(lo_done, PLACE["w", n0 + 1] + 1), (lo_done, PLACE["m", 7] + 1), (m15_lo, 1)]])

            def out_round(m):
                for s in range(3):
                    at = [R_OUT + 2 * s + half for half in range(2)]
                    ready = [[(lo_done, 6 * m + x)] for x in at]
                    out_block((1 + s) % RING, (2 + 2 * s) % RING, 3 * m + (evac0 + 1 + s), ready)

            with pe.Fori(0, 5) as m:
                out_round(m)
            pe.wait_ge(racc_done, NBLK3 - 1)
            for n in range(4):
                nc.tensor.matmul(tr_ps[0][:, n:n + 1], racc[:, n * P:(n + 1) * P], ones[:, 0:1], start=n == 0, stop=False,
                                 skip_group_check=True)
            pe.wait_ge(rsq_done, NBLK3)
            for n in range(4):
                end = nc.tensor.matmul(tr_ps[0][:, n:n + 1], rsq[(NBLK3 - 1) % RING][:, n * P:(n + 1) * P], ones[:, 0:1],
                                       start=False, stop=True, skip_group_check=True)
            end.then_inc(ss_done, 1)
            pe.wait_ge(fcol_done, 1)
            for n in range(4):
                end = nc.tensor.matmul(o_ps[:, n * P:(n + 1) * P], fcol[:, n:n + 1].to_broadcast([P, P]), ident[:, :],
                                       start=True, stop=True)
            end.then_inc(frstd_ps, 1)

        @block.scalar
        def _(act):
            act.preload_act_table(ACT.Exp)
            act.dma_start(lam_in[:, :], lam_d).then_inc(lam_ones_in, 16)
            act.dma_start(ones[:, :], const_d[:, C_ONE:C_ONE + P]).then_inc(lam_ones_in, 16)
            for b in range(3):
                act.sem_inc(y_stored[b], 16)
            act.sem_inc(m_stored, 16)

            def split_hi(slot_raw, slot_w, used, loads):
                act.wait_ge(raw_in[slot_raw], 16 * loads)
                act.wait_ge(pe_used, used)
                nc.scalar.activation(w_hi[slot_w][:, :], raw[slot_raw][:, :], ACT.Copy).then_inc(hi_done, 1)

            def split_hi_pair(slot_raw, dst, item, loads):
                act.wait_ge(raw_in[slot_raw], 16 * loads)
                nc.scalar.activation(dst[:, 2 * item:2 * item + 2, :].rearrange("p t q -> p (t q)"),
                                     raw[slot_raw][:, :], ACT.Copy).then_inc(hi_done, 1)

            def split_1(i, t):
                split_hi(t % RING, t % RING, NHU1 * i + (t + RING + 1), (NHU1 // RING) * i + (t // RING + 2))

            def square_x(k):
                act.wait_ge(xl_done, k + 1)
                nc.scalar.activation(x_raw[:, k, :], x_raw[:, k, :], ACT.Square).then_inc(xsq_done, 1)

            act.wait_ge(cols_in, 16)
            for k in range(KT):
                if k in SPLIT_AT:
                    n = SPLIT_AT.index(k)
                    split_hi(n, n, n + 1, 1)
                act.wait_ge(x_in[[k0 + n > k for k0, n in X_LOADS].index(True)], 16)
                nc.scalar.activation(act_hi[:, k, :], x_raw[:, k, :], ACT.Copy, scale=cols[:, S_G + k:S_G + k + 1]).then_inc(xh_done, 1)
                if k == 6:
                    act.wait_ge(lam_sum, 1)
                    nc.scalar.activation(lam_s[0:1, 2:4], lam_s[0:1, 0:2], ACT.Exp).then_inc(lam_exp, 1)
            split_1(0, 0)
            for k in SQ_SCALAR:
                square_x(k)

            def root_of_mean():
                act.wait_ge(ss_done, 1)
                nc.scalar.activation(rstd[:, :], o_ps[:, :], ACT.Sqrt, scale=1.0 / D, bias=eps[:, :]).then_inc(std_done, 1)

            def exps(i, idx, tile, spans, scale):
                act.wait_ge(biased, 8 * i + (idx + 1))
                for m, (lo, hi) in enumerate(spans):
                    end = nc.scalar.activation(tile[:, lo:hi], tile[:, lo:hi], ACT.Exp, scale=scale,
                                               bias=nmax[:, m:m + 1], accum_out=sums[:, m:m + 1])
                end.then_inc(exp_done, 1)

            def turned(i, idx, dst, n):
                assert idx in TURN_SPLIT
                act.wait_ge(t_ready, 16 * i + (idx + 1))
                nc.scalar.activation(dst, tr_ps[idx % 2][:, 0:n * P].rearrange("p (n q) -> p n q", n=n),
                                     ACT.Copy).then_inc(t_hi, 1)

            def split_block(i, w):
                act.wait_ge(evac_done, NBLK1 * i + (RING + w + 1))
                nc.scalar.activation(qk_hi[w][:, :], blk[w][:, :], ACT.Copy).then_inc(qh_done, 1)

            def tanh_half(i, w):
                act.wait_ge(evac_done, NBLK1 * i + (RING + w + 1))
                nc.scalar.activation(th[:, :], blk[w][:, :], ACT.Tanh, scale=0.5).then_inc(th_ready, 1)

            def store_y(i, b, tile):
                act.dma_start(y_dram[bass.ds(i + HEADS * b, 1), :, :].rearrange("o p q -> p (o q)"), tile[:, :]).then_inc(y_stored[b], 16)

            def head(i):
                first = isinstance(i, int)
                for w in range(NBLK1):
                    if not (first and w < 2):
                        split_1(i, 2 * w)
                    if first and w == 0:
                        split_1(i, 1)
                        split_1(i, 2)
                        root_of_mean()
                    if w == 12:
                        turned(i, TURN_V[0], v_hi[:, :, :], 4)
                    if w in SPLIT:
                        split_block(i, w)
                    if not (first and w == 0):
                        split_1(i, 2 * w + 1)
                    if w == 3:
                        turned(i, 0, v_hi[:, :, :], 4)
                    if 3 <= w < 7:
                        q = w - 3
                        turned(i, 1 + q, pt_a[0][:, 0:q + 1, q * P:(q + 1) * P], q + 1)
                    if 11 <= w < 15:
                        c = w - 11
                        turned(i, TURN_P[c], pt_b[0][:, :, c, :], 4)
                    if 2 <= w < 6:
                        q = w - 2
                        exps(i, q, sc, [(m * T, m * T + P * (q + 1)) for m in range(2)], SCALE_A)
                    if 10 <= w < 14:
                        exps(i, 4 + w - 10, sc, [(0, 6 * P)], SCALE_B)
                    if w in (AZ, BZ, CZ):
                        tanh_half(i, w)
                    if w == 7:
                        act.wait_ge(o_free, 2 * i + 2)
                        nc.scalar.activation(sq_a[:, :], o_a[:, :], ACT.Square)
                        nc.scalar.activation(sq_hi[:, :], o_a[:, :], ACT.Square).then_inc(sq_ready, 1)
                    if w == 8:
                        act.wait_ge(s_free, 9 * i + 6)
                        nc.scalar.activation(inv_a[:, :], sq_a[:, :], ACT.Sqrt).then_inc(sd_ready, 1)
                    if w == 9:
                        act.wait_ge(y_ready, 2 * i + 1)
                        store_y(i, 0, y_a)
                    if w == 15:
                        act.wait_ge(o_free, 2 * i + 3)
                        store_y(i, 1, y_b)
                    if w == CZ:
                        act.wait_ge(y_ready, 2 * i + 2)
                        store_y(i, 2, y_c)

            head(0)
            with act.Fori(1, HEADS) as i:
                head(i)

            def tanh_gate(done, b, col):
                act.wait_ge(evac_done, done)
                nc.scalar.activation(gate[b][:, :], gate[b][:, :], ACT.Tanh, scale=0.5, bias=col).then_inc(gate_done, 1)

            evac0 = NBLK1 * HEADS + RING

            r = W1 + RING
            for t, tick in enumerate(first_merged_ring()):
                for kind, n in tick:
                    if kind == "y":
                        split_hi_pair(r % RING, y_hi, n, r // RING + 1)
                    else:
                        split_hi(r % RING, n % RING, n + 1, r // RING + 1)
                    r += 1
                if t in (1, 3, 5):
                    b = t // 2
                    tanh_gate(evac0 + b + 1, b, cols[:, S_GB + b:S_GB + b + 1])
            act.wait_ge(m_ready, 1)
            act.dma_start(m_dram[0, :, :], merged[:, :]).then_inc(m_stored, 16)
            with act.Fori(1, KT - 1) as j:
                for t in range(NHU2):
                    split_hi(t % RING, t % RING, NHU2 * j + (W1 + RING + t + 1),
                             (NHU2 // RING) * j + ((W1 + N_Y + RING + t) // RING + 1))
                    if t in (1, 3, 5):
                        b = t // 2
                        tanh_gate(NBLK2 * j + (evac0 + b + 1), b, cols[:, bass.ds(3 * j + (S_GB + b), 1)])
                act.wait_ge(m_ready, j + 1)
                act.dma_start(m_dram[bass.ds(j, 1), :, :].rearrange("o p q -> p (o q)"), merged[:, :]).then_inc(m_stored, 16)
            r = R_LAST
            for t, tick in enumerate(last_merged_ring()):
                for kind, n in tick:
                    if kind == "w":
                        split_hi(r % RING, n % RING, n + 1, r // RING + 1)
                    elif n < N_M - 1:
                        split_hi_pair(r % RING, act_hi, n, r // RING + 1)
                    else:
                        act.wait_ge(raw_in[r % RING], 16 * (r // RING + 1))
                        nc.scalar.activation(act_hi[:, KT - 2, :], raw[r % RING][:, 0:T], ACT.Copy).then_inc(hi_done, 1)
                    r += 1
                if t in (1, 3, 5):
                    b = t // 2
                    tanh_gate(NBLK2 * (KT - 1) + evac0 + b + 1, b, cols[:, S_GB + 45 + b:S_GB + 46 + b])
            act.wait_ge(m_stored, 16 * KT)
            act.wait_ge(pe_used, W1 + W2 + RING)
            act.dma_start(res[:, :, :], x_t.rearrange("k p t -> p k t")).then_inc(res_in, 16)
            act.preload_act_table(ACT.Sqrt)
            act.wait_ge(m_ready, KT)
            nc.scalar.activation(act_hi[:, KT - 1, :], merged[:, :], ACT.Copy).then_inc(m15_hi, 1)
            r, n = R_OUT, W1 + W2 + RING

            def split_3(m, t):
                a, b = r + 2 + t, n + 2 + t
                split_hi(a % RING, b % RING, 6 * m + (b + 1), 2 * m + (a // RING + 1))

            def square_out(evac, k, s, rounds):
                if isinstance(k, int):
                    x_k, g_k = res[:, k, :], cols[:, S_FG + k:S_FG + k + 1]
                else:
                    x_k = res[:, bass.ds(k, 1), :].rearrange("p o q -> p (o q)")
                    g_k = cols[:, bass.ds(k + S_FG, 1)]
                if rounds is not None:
                    act.wait_ge(racc_done, rounds)
                act.wait_ge(evac_done, evac)
                nc.scalar.activation(rsq[s][:, :], x_k, ACT.Square).then_inc(rsq_done, 1)
                act.wait_ge(rsq_done, k + 1)
                nc.scalar.activation(x_k, x_k, ACT.Copy, scale=g_k).then_inc(rg_done, 1)

            evac1 = NBLK1 * HEADS + NBLK2 * KT + RING
            for t in range(2):
                a, b = r + t, n + t
                split_hi(a % RING, b % RING, b + 1, a // RING + 1)
            square_out(evac1 + 1, 0, 0, None)

            def out_round(m, splits):
                for s in range(3):
                    for half in range(2):
                        if 2 * s + half < splits:
                            split_3(m, 2 * s + half)
                    k = 3 * m + (1 + s)
                    square_out(3 * m + (evac1 + 2 + s), k, (1 + s) % RING,
                               None if isinstance(m, int) and k < RING else 3 * m + (s - 1))

            out_round(0, 6)
            with act.Fori(1, 4) as m:
                out_round(m, 6)
            out_round(4, 3)
            act.wait_ge(ss_done, 2)
            nc.scalar.activation(fcol[:, :], tr_ps[0][:, 0:4], ACT.Sqrt, scale=1.0 / D, bias=eps[:, :]).then_inc(std_done, 1)
            act.wait_ge(frstd_ps, 1)
            nc.scalar.activation(frstd[:, :], o_ps[:, :], ACT.Copy).then_inc(frstd_done, 1)
            for n, k in enumerate(BY_VECTOR):
                act.wait_ge(fin_ready, n + 1)
                act.dma_start(out_d[k, :, :], res[:, k, :]).then_inc(out_stored, 16)

        @block.vector
        def _(dve):
            steps = {"base": 0, "n": 0, "i": 0, "per": 0}

            def link(ins):
                steps["n"] += 1
                ins.then_inc(dve_step, 1)
                done = steps["base"] + steps["n"]
                dve.wait_ge(dve_step, steps["per"] * steps["i"] + done if steps["per"] else done)

            def enter(i, per):
                steps.update(i=i, per=per, base=steps["base"] + steps["n"], n=0)

            def leave(count):
                assert steps["n"] == steps["per"], steps
                steps.update(base=steps["base"] + steps["per"] * count, n=0, i=0, per=0)

            tt, ts, stt = nc.vector.tensor_tensor, nc.vector.tensor_scalar, nc.vector.scalar_tensor_tensor
            dve.sem_inc(evac_done, RING)
            dve.sem_inc(s_free, 1)
            dve.sem_inc(o_free, 1)
            dve.sem_inc(t_free, 2)
            nc.vector.memset(eps[:, :], EPS)

            def split_lo(slot_raw, slot_w, hi):
                dve.wait_ge(hi_done, hi)
                tt(w_lo[slot_w][:, :], raw[slot_raw][:, :], w_hi[slot_w][:, :].bitcast(f32), ALU.subtract).then_inc(lo_done, 1)

            def split_lo_pair(slot_raw, lo, hi_part, item, hi):
                dve.wait_ge(hi_done, hi)
                tt(lo[:, 2 * item:2 * item + 2, :].rearrange("p t q -> p (t q)"), raw[slot_raw][:, :],
                   hi_part[:, 2 * item:2 * item + 2, :].rearrange("p t q -> p (t q)").bitcast(f32), ALU.subtract).then_inc(lo_done, 1)

            def split_1(i, t):
                split_lo(t % RING, t % RING, NHU1 * i + (t + RING + 1))

            def x_low(k):
                dve.wait_ge(xh_done, k + 1)
                stt(act_lo[:, k, :], x_raw[:, k, :], cols[:, S_G + k:S_G + k + 1], act_hi[:, k, :].bitcast(f32),
                    ALU.mult, ALU.subtract).then_inc(xl_done, 1)

            def add_squares_x(k):
                n = (SQ_VECTOR + SQ_SCALAR).index(k)
                if k in SQ_VECTOR:
                    link(tt(xacc[:, :] if n == 0 else x_raw[:, k, :], x_raw[:, k, :], x_raw[:, k, :], ALU.mult))
                else:
                    dve.wait_ge(xsq_done, SQ_SCALAR.index(k) + 1)
                if n > 1:
                    dve.wait_ge(xacc_add, n - 1)
                if n:
                    tt(xacc[:, :], xacc[:, :], x_raw[:, k, :], ALU.add).then_inc(xacc_add, 1)

            dve.wait_ge(cols_in, 16)
            for k in range(KT):
                if k in SPLIT_AT:
                    n = SPLIT_AT.index(k)
                    split_lo(n, n, n + 1)
                x_low(k)
                if k == 3:
                    dve.wait_ge(lam_ones_in, 16 * 2)
                    lam_v = lam_in[:, :].rearrange("o (a b d) -> o a b d", a=2, b=2)
                    link(tt(lam_w[:, :].rearrange("o (a d) -> o a d", a=2), lam_v[:, :, 0, :], lam_v[:, :, 1, :], ALU.mult))
                    nc.vector.reduce_sum(lam_s[:, 0:2], lam_w[:, :].rearrange("o (a d) -> o a d", a=2), AX.X).then_inc(lam_sum, 1)
                    ts(gsub[:, :], cols[:, S_SUB:S_SUB + 1], 1.0 - LAM_INIT, None, ALU.mult)
                    link(ts(cols[:, S_GB:S_GB + 48], cols[:, S_GB:S_GB + 48], 0.5, None, ALU.mult))
                if k == 8:
                    dve.wait_ge(lam_exp, 1)
                    link(tt(lam_s[:, 6:7], lam_s[:, 2:3], lam_s[:, 3:4], ALU.subtract))
                    ts(lam_s[:, 4:5], lam_s[:, 6:7], LAM_INIT, None, ALU.add).then_inc(lam_set, 1)
            split_1(0, 0)
            for k in SQ_VECTOR + SQ_SCALAR:
                add_squares_x(k)
            dve.wait_ge(xacc_add, X_ADDS - 1)
            dve.wait_ge(pool_add, len(SQ_POOL) - 1)
            tt(xacc[:, :], xacc[:, :], xacc_pool[:, :], ALU.add).then_inc(xacc_add, 1)

            def reciprocal_root():
                dve.wait_ge(std_done, 1)
                nc.vector.memset(u[:, 0:2], 0.0)
                nc.vector.tensor_copy(ones_r[:, :], ones[:, :])
                link(nc.vector.reciprocal(rstd[:, :], rstd[:, :]))
                dve.wait_ge(lam_bc, 1)
                nc.vector.tensor_copy(lam_col[:, :], tr_ps[0][:, 0:1])

            classed = {Q0, Q1, K1, Q2, K2, V1, V2}

            def scale_block(i, w):
                late = isinstance(i, int) and w == 0
                dve.wait_ge(pe_used, NHU1 * i + (2 * w + 2 + late + RING))
                if w in classed:
                    ins = tt(as_class(blk[w][:, :]), by_class(pb[w % RING][:, :]), by_class(rstd[:, :]), ALU.mult)
                else:
                    ins = tt(blk[w][:, :], pb[w % RING][:, :], rstd[:, :], ALU.mult)
                ins.then_inc(evac_done, 1)

            def bias_a(i, q):
                n = P * (q + 1)
                dve.wait_ge(s_ready, 9 * i + (q + 1))
                if q:
                    dve.wait_ge(p_ready, 8 * i + q)
                for m in range(2):
                    end = stt(sc_a[:, m, 0:n], masks[:, C_MA + T - n:C_MA + T], slope[:, 0:1], sc_ps[m][:, 0:n], ALU.mult, ALU.add)
                end.then_inc(s_free, 1)
                dve.wait_ge(s_free, 9 * i + (q + 2))
                link(nc.vector.reduce_max(rsum[:, :], sc_a[:, :, 0:n], AX.X))
                ts(nmax[:, :], rsum[:, :], -SCALE_A, None, ALU.mult).then_inc(biased, 1)

            def norm_a(i, q):
                n = P * (q + 1)
                dve.wait_ge(exp_done, 8 * i + (q + 1))
                link(nc.vector.reciprocal(rsum[:, :], sums[:, :]))
                link(tt(rsum[:, 1:2], rsum[:, 1:2], lam_col[:, :], ALU.mult))
                link(ts(tmp_a[:, 0:n], sc_a[:, 1, 0:n], rsum[:, 1:2], None, ALU.mult))
                stt(pr[:, 0:n], sc_a[:, 0, 0:n], rsum[:, 0:1], tmp_a[:, 0:n], ALU.mult, ALU.subtract).then_inc(p_ready, 1)

            def bias_b(i, c):
                dve.wait_ge(s_ready, 9 * i + (6 + c))
                if c:
                    dve.wait_ge(p_ready, 8 * i + (4 + c))
                m0 = C_M0 + 3 - c
                stt(sc[:, 0:T], masks[:, m0:m0 + T], slope[:, 1:2], sc_ps[0][:, :], ALU.mult, ALU.add)
                for g in (1, 2):
                    end = stt(sc[:, (3 + g) * P:(4 + g) * P], masks[:, C_M12 + (g - 1) * P:C_M12 + g * P],
                              slope[:, 1 + g:2 + g], sc_ps[1][:, (g - 1) * P:g * P], ALU.mult, ALU.add)
                end.then_inc(s_free, 1)
                dve.wait_ge(s_free, 9 * i + (7 + c))
                link(nc.vector.reduce_max(rsum[:, 0:1], sc[:, 0:6 * P], AX.X))
                ts(nmax[:, 0:1], rsum[:, 0:1], -SCALE_B, None, ALU.mult).then_inc(biased, 1)

            def norm_b(i, c):
                dve.wait_ge(exp_done, 8 * i + (5 + c))
                link(nc.vector.reciprocal(rsum[:, 0:1], sums[:, 0:1]))
                ts(pr[:, :], sc[:, 0:6 * P], rsum[:, 0:1], None, ALU.mult).then_inc(p_ready, 1)

            def turned(i, idx, hi_part, dst, n):
                dve.wait_ge(t_hi, len(TURN_SPLIT) * i + (TURN_SPLIT.index(idx) + 1))
                tt(dst, tr_ps[idx % 2][:, 0:n * P].rearrange("p (n q) -> p n q", n=n), hi_part.bitcast(f32),
                   ALU.subtract).then_inc(t_free, 1)

            def turned_whole(i, idx, dst, n):
                dve.wait_ge(t_ready, 16 * i + (idx + 1))
                nc.vector.tensor_copy(dst, tr_ps[idx % 2][:, 0:n * P].rearrange("p (n q) -> p n q", n=n)).then_inc(t_free, 1)

            def split_block(i, w):
                dve.wait_ge(qh_done, len(SPLIT) * i + (SPLIT.index(w) + 1))
                tt(qk_lo[w][:, :], blk[w][:, :], qk_hi[w][:, :].bitcast(f32), ALU.subtract).then_inc(ql_done, 1)

            def silu(i, idx, w):
                dve.wait_ge(th_ready, 3 * i + (idx + 1))
                link(stt(blk[w][:, :], th[:, :], 1.0, blk[w][:, :], ALU.add, ALU.mult))

            def head(i):
                first = isinstance(i, int)
                link(nc.vector.tensor_copy(slope[:, :], slopes[:, bass.ds(4 * i, 4)]))
                link(nc.vector.tensor_copy(taps[:, :], cols[:, bass.ds(3 * i + S_CONV, 3)]))
                for w in range(NBLK1):
                    if 3 <= w < 7:
                        norm_a(i, w - 3)
                    if 11 <= w < 15:
                        norm_b(i, w - 11)
                    if not (first and w < 2):
                        split_1(i, 2 * w)
                    if first and w == 0:
                        split_1(i, 1)
                        split_1(i, 2)
                        reciprocal_root()
                    if w == 4:
                        silu(i, 0, AZ)
                    if w == 12:
                        turned(i, TURN_V[0], v_hi[:, :, :], v_lo[:, :, :], 4)
                    if w in (13, 14):
                        turned_whole(i, TURN_V[w - 12], v_g[w - 12][:, :, :], 4)
                    if w == 14:
                        silu(i, 1, BZ)
                    if w == 9:
                        dve.wait_ge(sd_ready, i + 1)
                        link(nc.vector.reciprocal(inv_a[:, :], inv_a[:, :]))
                        link(stt(o_a[:, :], o_a[:, :], gsub[:, :], inv_a[:, :], ALU.mult, ALU.mult))
                        dve.wait_ge(y_stored[0], 16 * i + 16)
                        stt(y_a[:, :], o_a[:, :], 0.5, blk[AZ][:, :], ALU.mult, ALU.mult).then_inc(y_ready, 1)
                    scale_block(i, w)
                    if not (first and w == 0):
                        split_1(i, 2 * w + 1)
                    if w in SPLIT:
                        split_block(i, w)
                    if 2 <= w < 6:
                        bias_a(i, w - 2)
                    if 10 <= w < 14:
                        bias_b(i, w - 10)
                    if w == 3:
                        turned(i, 0, v_hi[:, :, :], v_lo[:, :, :], 4)
                    if 3 <= w < 7:
                        q = w - 3
                        turned(i, 1 + q, *[t[:, 0:q + 1, q * P:(q + 1) * P] for t in pt_a], q + 1)
                    if 11 <= w < 15:
                        c = w - 11
                        turned(i, TURN_P[c], *[t[:, :, c, :] for t in pt_b], 4)
                        turned_whole(i, TURN_P[c] + 1, pt_g[:, :, c, :], 2)
                    if w == 7:
                        dve.wait_ge(o_ready, 2 * i + 1)
                        nc.vector.tensor_copy(o_a[:, :], o_ps[:, :]).then_inc(o_free, 1)
                        dve.wait_ge(sq_ready, i + 1)
                        tt(sq_lo[:, :], sq_a[:, :], sq_hi[:, :].bitcast(f32), ALU.subtract).then_inc(sq_split, 1)
                    if w == 8:
                        dve.wait_ge(s_ready, 9 * i + 5)
                        ts(sq_a[:, :], sc_ps[0][:, :], 1.0 / P, EPS, ALU.mult, ALU.add).then_inc(s_free, 1)
                    if w == 15:
                        dve.wait_ge(o_ready, 2 * i + 2)
                        dve.wait_ge(y_stored[1], 16 * i + 16)
                        dve.wait_ge(y_stored[2], 16 * i + 16)
                        stt(y_b[:, :].rearrange("p (b c) -> p b c", c=4), o_ps[:, :].rearrange("p (c b) -> p b c", c=4), 0.5,
                            blk[BZ][:, :].rearrange("p (b c) -> p b c", c=4), ALU.mult, ALU.mult).then_inc(o_free, 1)
                    if w == CX:
                        dve.wait_ge(evac_done, NBLK1 * i + (RING + CX + 1))
                        link(tt(u[:, 2:T + 2], blk[CC][:, :], blk[CX][:, :], ALU.mult))
                        link(ts(blk[CC][:, :], u[:, 2:T + 2], taps[:, 2:3], None, ALU.mult))
                        link(stt(blk[CC][:, :], u[:, 1:T + 1], taps[:, 1:2], blk[CC][:, :], ALU.mult, ALU.add))
                        link(stt(blk[CC][:, :], u[:, 0:T], taps[:, 0:1], blk[CC][:, :], ALU.mult, ALU.add))
                        link(tt(blk[CC][:, :], blk[CC][:, :], blk[CB][:, :], ALU.mult))
                    if w == CZ:
                        silu(i, 2, CZ)
                        dve.wait_ge(y_stored[2], 16 * i + 16)
                        dve.wait_ge(y_stored[1], 16 * i + 32)
                        stt(y_c[:, :], blk[CC][:, :], 0.5, blk[CZ][:, :], ALU.mult, ALU.mult).then_inc(y_ready, 1)

            dve.wait_ge(const_in, 16 * 3)
            before = steps["n"]
            head(0)
            links = steps["n"] - before - 1
            with dve.Fori(1, HEADS) as i:
                enter(i - 1, links)
                head(i)
                leave(HEADS - 1)

            def merge(j, t, used, gates):
                if t in (1, 3, 5):
                    b = t // 2
                    dve.wait_ge(pe_used, used)
                    tt(gate[b][:, :], pb[b][:, :], rstd[:, :], ALU.mult).then_inc(evac_done, 1)
                if t >= 6:
                    b = t - 6
                    dve.wait_ge(pe_used, used)
                    dve.wait_ge(gate_done, gates)
                    stt(gate[b][:, :], gate[b][:, :], 1.0, pb[b][:, :], ALU.add, ALU.mult).then_inc(evac_done, 1)
                    if b == 1:
                        dve.wait_ge(evac_done, NBLK2 * j + (NBLK1 * HEADS + RING + 5))
                        link(tt(gate[0][:, :], gate[0][:, :], gate[1][:, :], ALU.add))
                    if b == 2:
                        dve.wait_ge(evac_done, NBLK2 * j + (NBLK1 * HEADS + RING + 6))
                        dve.wait_ge(m_stored, 16 * j + 16)
                        tt(merged[:, :], gate[0][:, :], gate[2][:, :], ALU.add).then_inc(m_ready, 1)

            n_last = W1 + (KT - 1) * NHU2
            r = W1 + RING
            for t, tick in enumerate(first_merged_ring()):
                for kind, n in tick:
                    if kind == "y":
                        split_lo_pair(r % RING, y_lo, y_hi, n, r + 1)
                    else:
                        split_lo(r % RING, n % RING, r + 1)
                    r += 1
                if t == 1:
                    for b in range(3):
                        dve.wait_ge(y_stored[b], 16 * (HEADS + 1))
                merge(0, t, W1 + RING + t + 1, 3)
            with dve.Fori(1, KT - 1) as j:
                enter(j - 1, 1)
                for t in range(NHU2):
                    split_lo(t % RING, t % RING, NHU2 * j + (W1 + N_Y + RING + t + 1))
                    merge(j, t, NHU2 * j + (W1 + RING + t + 1), 3 * j + 3)
                leave(KT - 2)
            r = R_LAST
            for t, tick in enumerate(last_merged_ring()):
                if t >= 6:
                    merge(KT - 1, t, n_last + RING + t + 1, 3 * KT)
                for kind, n in tick:
                    if kind == "w":
                        split_lo(r % RING, n % RING, r + 1)
                    elif n < N_M - 1:
                        split_lo_pair(r % RING, act_lo, act_hi, n, r + 1)
                    else:
                        dve.wait_ge(hi_done, r + 1)
                        tt(act_lo[:, KT - 2, :], raw[r % RING][:, 0:T], act_hi[:, KT - 2, :].bitcast(f32),
                           ALU.subtract).then_inc(lo_done, 1)
                    r += 1
                if t < 6:
                    merge(KT - 1, t, n_last + RING + t + 1, 3 * KT)
            dve.wait_ge(m15_hi, 1)
            tt(act_lo[:, KT - 1, :], merged[:, :], act_hi[:, KT - 1, :].bitcast(f32), ALU.subtract).then_inc(m15_lo, 1)
            r, n = R_OUT, W1 + W2 + RING

            def add_residual(used, bank, blk_i):
                dve.wait_ge(pe_used, used)
                x_i = res[:, blk_i, :] if isinstance(blk_i, int) else res[:, bass.ds(blk_i, 1), :].rearrange("p o q -> p (o q)")
                stt(x_i, pb[bank][:, :], 0.5, x_i, ALU.mult, ALU.add).then_inc(evac_done, 1)

            for t in range(2):
                split_lo((r + t) % RING, (n + t) % RING, r + t + 1)
            dve.wait_ge(res_in, 16)
            add_residual(n + 2, 0, 0)

            def out_round(m, splits):
                for s in range(3):
                    for half in range(2):
                        t = 2 * s + half
                        if t < splits:
                            split_lo((r + 2 + t) % RING, (n + 2 + t) % RING, 6 * m + (r + 2 + t + 1))
                    add_residual(6 * m + (n + 2 + 2 * s + 2), (1 + s) % RING, 3 * m + (1 + s))

            with dve.Fori(0, 4) as m:
                out_round(m, 6)
            out_round(4, 3)
            dve.wait_ge(std_done, 2)
            nc.vector.reciprocal(fcol[:, :], fcol[:, :]).then_inc(fcol_done, 1)
            dve.wait_ge(frstd_done, 1)
            for k in BY_VECTOR:
                tt(res[:, k, :], res[:, k, :], frstd[:, :], ALU.mult).then_inc(fin_ready, 1)


def kernel(**inputs):
    import numpy as np
    import concourse.bacc as bacc
    from concourse.bass_utils import run_bass_kernel_spmd

    def get(name):
        return np.ascontiguousarray(inputs[name])

    const = np.zeros((P, C_END), np.float32)
    p = np.arange(P)[:, None]
    dist = p + (T - P) - np.arange(T)[None, :]
    const[:, C_MA:C_MA + T] = np.where(dist >= 0, dist, FAR)
    dist = 4 * p + 3 - np.arange(515)[None, :]
    const[:, C_M0:C_M0 + 515] = np.where((dist >= 0) & (dist <= 128), dist, FAR)
    dist = 4 * (p - np.arange(P)[None, :])
    const[:, C_M12:C_M12 + P] = np.where(dist >= 0, dist, FAR)
    const[:, C_M12 + P:C_M12 + 2 * P] = np.where((dist >= 0) & (dist % 16 == 0), dist, FAR)
    const[:, C_ID:C_ID + P] = np.eye(P)
    const[:, C_ONE:C_ONE + P] = 1.0
    slopes = 2.0 ** (-8.0 * np.arange(1, 4 * HEADS + 1) / (4 * HEADS))
    for h in range(HEADS):
        const[:, C_SL + 4 * h] = -slopes[h] / SCALE_A
        for g in range(3):
            const[:, C_SL + 4 * h + 1 + g] = -slopes[HEADS + g * HEADS + h] / SCALE_B

    def units(w, half):
        return w[half * 8 * P:(half + 1) * 8 * P].reshape(8, P, -1, P).transpose(2, 1, 0, 3).reshape(-1, P, HU)

    w_in = get("w_in")[0]
    wi = [units(w_in, half) for half in range(2)]
    wb = [units(get(f"w_branch_{x}")[0], 0) for x in "abc"]
    wo = [units(get("w_out")[0], half) for half in range(2)]
    nb = HEADS
    order = [0, nb, 2 * nb, 3 * nb]
    b0 = 4 * nb
    order += [b0, b0 + nb, b0 + 3 * nb, b0 + 4 * nb, b0 + 6 * nb, b0 + 7 * nb]
    order += [b0 + 2 * nb, b0 + 5 * nb, b0 + 8 * nb, b0 + 9 * nb]
    c0 = b0 + 10 * nb
    order += [c0, c0 + nb, c0 + 2 * nb, c0 + 3 * nb]
    g0 = c0 + 4 * nb
    wst = np.empty((W1 + W2 + W3, P, HU), np.float32)
    n = 0
    for h in range(HEADS):
        for b in order:
            for half in range(2):
                wst[n] = wi[half][b + h]
                n += 1
    for n_first, (w, half) in enumerate(FIRST_UNITS):
        wst[n_first] = wi[half][order[w]]
    for j in range(KT):
        for b in range(3):
            for half in range(2):
                wst[n] = wi[half][g0 + b * KT + j]
                n += 1
        for b in range(3):
            wst[n] = wb[b][j]
            n += 1
    for j in range(NBLK3):
        for half in range(2):
            wst[n] = wo[half][j]
            n += 1

    x_t = np.ascontiguousarray(get("x")[0].T).reshape(KT, P, T)
    cols = np.concatenate([
        get("norm_g")[0].reshape(KT, P).T,
        get("gate_b")[0].reshape(3, KT, P).transpose(2, 1, 0).reshape(P, 48),
        get("subln_g")[0].reshape(P, 1),
        get("conv_w")[0].reshape(3, HEADS, P).transpose(2, 1, 0).reshape(P, 24),
        get("final_g").reshape(KT, P).T], axis=1)
    lam = np.stack([get(f"lambda_{x}")[0] for x in ("q1", "k1", "q2", "k2")]).reshape(1, 256)
    arrays = {"wst": wst, "x_t": x_t, "cols_d": np.ascontiguousarray(cols), "lam_d": lam, "const_d": const}

    nc = bacc.Bacc("TRN2", target_bir_lowering=False, num_devices=1)
    args = [nc.dram_tensor(k, a.shape, mybir.dt.from_np(a.dtype), kind="ExternalInput").ap() for k, a in arrays.items()]
    args.append(nc.dram_tensor("out_0", (KT, P, T), mybir.dt.float32, kind="ExternalOutput").ap())
    program(nc, *args)
    r = run_bass_kernel_spmd(nc, [arrays], core_ids=[0])
    return r.results[0]["out_0"].reshape(D, T).T.reshape(1, T, D)
```
